# Optimizing a Trainium2 kernel written in Bass

```python
import math
import jax, jax.numpy as jnp
from jax import lax
import numpy as np

D_MODEL = 1024
BATCH = 1
SEQ = 256
DEPTH = 1

RET_HEADS = 4
RET_QK_DIM = 64
RET_V_DIM = 128
RET_CHUNK = 128
RET_WIDTH = RET_HEADS * RET_V_DIM
MOBA_HEADS = 8
MOBA_HEAD_DIM = 64
MOBA_WIDTH = MOBA_HEADS * MOBA_HEAD_DIM
MOBA_BLOCK = 256
MOBA_TOPK = 3
MOBA_QBLOCK = 64
REL_BUCKETS = 32
REL_MAX_DIST = 128
D_FF = -(-8 * D_MODEL // (3 * 256)) * 256
MIX_WIDTH = RET_WIDTH + MOBA_WIDTH
IN_COLS = 2 * RET_HEADS * RET_QK_DIM + 2 * RET_WIDTH + 3 * MOBA_WIDTH
EPS = 1e-6
ROPE_BASE = 10000.0

kernel_name = "hybrid_retention_moba_sandwich_block"

def rmsnorm(x, g):
    xf = x.astype(jnp.float32)
    y = xf * lax.rsqrt(jnp.mean(xf * xf, axis=-1, keepdims=True) + EPS)
    return (y * g.astype(jnp.float32)).astype(x.dtype)

def head_rmsnorm(x):
    xf = x.astype(jnp.float32)
    return (xf * lax.rsqrt(jnp.mean(xf * xf, axis=-1, keepdims=True) + EPS)).astype(x.dtype)

def rotary(x):
    s, d = x.shape[1], x.shape[-1]
    half = d // 2
    inv_freq = ROPE_BASE ** (-jnp.arange(half, dtype=jnp.float32) / half)
    ang = jnp.arange(s, dtype=jnp.float32)[:, None] * inv_freq[None, :]
    cos = jnp.cos(ang)[None, :, None, :]
    sin = jnp.sin(ang)[None, :, None, :]
    xf = x.astype(jnp.float32)
    x1, x2 = xf[..., :half], xf[..., half:]
    return jnp.concatenate([x1 * cos - x2 * sin, x2 * cos + x1 * sin], axis=-1).astype(x.dtype)

def t5_bucket(rel):
    n = jnp.maximum(rel, 0)
    max_exact = REL_BUCKETS // 2
    is_small = n < max_exact
    nf = jnp.maximum(n, 1).astype(jnp.float32)
    large = max_exact + (jnp.log(nf / max_exact) / math.log(REL_MAX_DIST / max_exact)
                         * (REL_BUCKETS - max_exact)).astype(jnp.int32)
    large = jnp.minimum(large, REL_BUCKETS - 1)
    return jnp.where(is_small, n, large)

def retention(q, k, v):
    b, s, h, dk = q.shape
    dv = v.shape[-1]
    c = RET_CHUNK
    n = s // c

    def to_chunks(t):
        return t.astype(jnp.float32).reshape(b, n, c, h, t.shape[-1]).transpose(1, 0, 3, 2, 4)

    qc, kc, vc = to_chunks(q), to_chunks(k), to_chunks(v)
    log_gamma = jnp.log1p(-jnp.exp(jnp.linspace(math.log(1.0 / 32), math.log(1.0 / 512), RET_HEADS)))
    log_gamma = log_gamma.astype(jnp.float32)
    idx = jnp.arange(c, dtype=jnp.float32)
    diff = idx[:, None] - idx[None, :]
    intra_decay = jnp.where(diff >= 0, jnp.exp(jnp.maximum(diff, 0.0)[None] * log_gamma[:, None, None]), 0.0)
    q_decay = jnp.exp((idx + 1.0)[None, :] * log_gamma[:, None])
    k_decay = jnp.exp((c - 1.0 - idx)[None, :] * log_gamma[:, None])
    chunk_decay = jnp.exp(c * log_gamma)

    def step(state, inp):
        qi, ki, vi = inp
        scores = jnp.einsum('bhid,bhjd->bhij', qi, ki) * intra_decay[None]
        o = jnp.einsum('bhij,bhje->bhie', scores, vi)
        o = o + jnp.einsum('bhid,bhde->bhie', qi * q_decay[None, :, :, None], state)
        new_state = state * chunk_decay[None, :, None, None] + jnp.einsum(
            'bhjd,bhje->bhde', ki * k_decay[None, :, :, None], vi)
        return new_state, o

    state0 = jnp.zeros((b, h, dk, dv), jnp.float32)
    _, o = lax.scan(step, state0, (qc, kc, vc))
    return o.transpose(1, 0, 3, 2, 4).reshape(b, s, h, dv).astype(v.dtype)

def moba_attention(q, k, v, rel_bias):
    b, s, h, d = q.shape
    bs = MOBA_BLOCK
    nb = -(-s // bs)
    sp = nb * bs
    pad = sp - s

    def prep(t):
        return jnp.pad(t, ((0, 0), (0, pad), (0, 0), (0, 0))).transpose(0, 2, 1, 3)

    q, k, v = prep(q), prep(k), prep(v)
    kb = k.reshape(b, h, nb, bs, d)
    vb = v.reshape(b, h, nb, bs, d)
    k_mean = jnp.mean(kb.astype(jnp.float32), axis=3)
    gate = jnp.einsum('bhsd,bhnd->bhsn', q.astype(jnp.float32), k_mean)
    q_blk = jnp.arange(sp) // bs
    fully_past = jnp.arange(nb)[None, :] < q_blk[:, None]
    gate = jnp.where(fully_past[None, None], gate, -jnp.inf)
    topk = min(MOBA_TOPK, nb)
    vals, sel = lax.top_k(gate, topk)
    valid = jnp.isfinite(vals)
    sel = jnp.where(valid, sel, 0)

    bias_t = rel_bias.T.astype(jnp.float32)
    scale = d ** -0.5
    bi = jnp.arange(b)[:, None, None, None]
    hi = jnp.arange(h)[None, :, None, None]
    kidx = jnp.arange(bs)

    def query_block(start):
        qs = lax.dynamic_slice_in_dim(q, start, MOBA_QBLOCK, axis=2)
        sel_b = lax.dynamic_slice_in_dim(sel, start, MOBA_QBLOCK, axis=2)
        valid_b = lax.dynamic_slice_in_dim(valid, start, MOBA_QBLOCK, axis=2)
        qp = start + jnp.arange(MOBA_QBLOCK)
        k_sel = kb[bi, hi, sel_b]
        v_sel = vb[bi, hi, sel_b]
        s_sel = jnp.einsum('bhqd,bhqnkd->bhqnk', qs, k_sel).astype(jnp.float32) * scale
        kp_sel = sel_b[..., None] * bs + kidx
        bias_sel = bias_t[hi[..., None], t5_bucket(qp[None, None, :, None, None] - kp_sel)]
        s_sel = jnp.where(valid_b[..., None], s_sel + bias_sel, -jnp.inf)
        own = start // bs
        k_own = lax.dynamic_index_in_dim(kb, own, axis=2, keepdims=False)
        v_own = lax.dynamic_index_in_dim(vb, own, axis=2, keepdims=False)
        s_own = jnp.einsum('bhqd,bhkd->bhqk', qs, k_own).astype(jnp.float32) * scale
        rel_own = qp[:, None] - (own * bs + kidx)[None, :]
        bias_own = bias_t[:, t5_bucket(rel_own)]
        s_own = jnp.where(rel_own[None, None] >= 0, s_own + bias_own[None], -jnp.inf)
        logits = jnp.concatenate([s_sel.reshape(b, h, MOBA_QBLOCK, topk * bs), s_own], axis=-1)
        p = jax.nn.softmax(logits, axis=-1).astype(v.dtype)
        p_sel = p[..., :topk * bs].reshape(b, h, MOBA_QBLOCK, topk, bs)
        p_own = p[..., topk * bs:]
        return (jnp.einsum('bhqnk,bhqnkd->bhqd', p_sel, v_sel)
                + jnp.einsum('bhqk,bhkd->bhqd', p_own, v_own))

    starts = jnp.arange(sp // MOBA_QBLOCK) * MOBA_QBLOCK
    o = lax.map(query_block, starts)
    o = o.transpose(1, 2, 0, 3, 4).reshape(b, h, sp, d)[:, :, :s]
    return o.transpose(0, 2, 1, 3)

def setup_inputs(seed: int = 0) -> dict:
    key = jax.random.key(seed)
    ks = jax.random.split(key, 12)
    f32 = jnp.float32

    def w(k, shape, fan_in):
        return jax.random.normal(k, shape, f32) * fan_in ** -0.5

    def gain(k):
        return 1.0 + 0.02 * jax.random.normal(k, (DEPTH, D_MODEL), f32)

    return {
        "x": jax.random.normal(ks[0], (BATCH, SEQ, D_MODEL), f32),
        "w_in": w(ks[1], (DEPTH, D_MODEL, IN_COLS), D_MODEL),
        "w_out": w(ks[2], (DEPTH, MIX_WIDTH, D_MODEL), MIX_WIDTH),
        "pre_mix_norm": gain(ks[3]),
        "post_mix_norm": gain(ks[4]),
        "pre_ffn_norm": gain(ks[5]),
        "post_ffn_norm": gain(ks[6]),
        "rel_bias": 0.5 * jax.random.normal(ks[7], (REL_BUCKETS, MOBA_HEADS), f32),
        "w_gate": w(ks[8], (DEPTH, D_MODEL, D_FF), D_MODEL),
        "w_up": w(ks[9], (DEPTH, D_MODEL, D_FF), D_MODEL),
        "w_down": w(ks[10], (DEPTH, D_FF, D_MODEL), D_FF),
    }

def reference(x, w_in, w_out, pre_mix_norm, post_mix_norm, pre_ffn_norm, post_ffn_norm,
              rel_bias, w_gate, w_up, w_down):
    b, s, _ = x.shape
    sizes = [RET_HEADS * RET_QK_DIM, RET_HEADS * RET_QK_DIM, RET_WIDTH, RET_WIDTH,
             MOBA_WIDTH, MOBA_WIDTH, MOBA_WIDTH]
    split_at = np.cumsum(sizes)[:-1].tolist()
    for layer in range(DEPTH):
        h = rmsnorm(x, pre_mix_norm[layer])
        proj = h @ w_in[layer]
        rq, rk, rv, rg, mq, mk, mv = jnp.split(proj, split_at, axis=-1)
        rq = rotary(rq.reshape(b, s, RET_HEADS, RET_QK_DIM))
        rk = rotary(rk.reshape(b, s, RET_HEADS, RET_QK_DIM)) * (RET_QK_DIM ** -0.5)
        rv = rv.reshape(b, s, RET_HEADS, RET_V_DIM)
        ret = head_rmsnorm(retention(rq, rk, rv)).reshape(b, s, RET_WIDTH)
        ret = jax.nn.silu(rg) * ret
        moba = moba_attention(mq.reshape(b, s, MOBA_HEADS, MOBA_HEAD_DIM),
                              mk.reshape(b, s, MOBA_HEADS, MOBA_HEAD_DIM),
                              mv.reshape(b, s, MOBA_HEADS, MOBA_HEAD_DIM),
                              rel_bias).reshape(b, s, MOBA_WIDTH)
        mix = jnp.concatenate([ret, moba], axis=-1) @ w_out[layer]
        x = x + rmsnorm(mix, post_mix_norm[layer])
        h = rmsnorm(x, pre_ffn_norm[layer])
        f = (jax.nn.silu(h @ w_gate[layer]) * (h @ w_up[layer])) @ w_down[layer]
        x = x + rmsnorm(f, post_ffn_norm[layer])
    return x


_drawn_inputs = setup_inputs


def setup_inputs(seed=0):
    import zlib

    import numpy as np

    out = dict(_drawn_inputs(seed))
    spreads = {}
    factors = {'post_mix_norm': 3.484, 'pre_ffn_norm': 3.235, 'post_ffn_norm': 4.753}
    for name, (base, spread) in spreads.items():
        noise = np.random.default_rng([zlib.crc32(name.encode()), seed]).standard_normal(out[name].shape)
        drawn = base * np.exp(spread * noise) if base else spread * noise
        out[name] = __import__('jax').numpy.asarray(drawn.astype(out[name].dtype))
    for name, factor in factors.items():
        out[name] = (out[name] * factor).astype(out[name].dtype)
    return out
```

```python
import math
from contextlib import ExitStack

import numpy as np

import concourse.bass as bass
from concourse import mybir

F32 = mybir.dt.float32
F32R = mybir.dt.float32r
ALU = mybir.AluOpType
ACT = mybir.ActivationFunctionType
AX_X = mybir.AxisListType.X

P = 128
D = 1024
S = 256
NT = S // P
NK = D // P
RH, RD, RV = 4, 64, 128
MH, MD = 8, 64
MB = MH * MD // P
IN_COLS = 2 * RH * RD + 2 * RH * RV + 3 * MH * MD
DFF = -(-8 * D // (3 * 256)) * 256
EPS = 1e-6
BUCKETS, MAX_DIST = 32, 128
CW = 512
UNIT = 1024

RQK_COL, RV_COL, RG_COL, MQ_COL, MK_COL, MV_COL = range(6)
ORDER = [MQ_COL, MK_COL, MV_COL, RQK_COL, RV_COL, RG_COL]
NG = IN_COLS // CW
UPG = NK * CW // UNIT
KPU = UNIT // CW
N_IN = NG * UPG
WOUT_K = [4, 5, 6, 7, 0, 1, 2, 3]
N_OUT = len(WOUT_K)
FG = 256
NF = DFF // FG
GU = NK * 2 * FG // UNIT
DN = FG * D // (P * UNIT)
PER = GU + DN

RAW = 6
RING = 8
DRING = 4
LEAD = 5
MASKED = 1e30
REV = 2 * P + S // 2

Q_T, K_T, S0, RQK_T = 5, 9, 10, 18
PT_LAG, PV_LAG = 2, 3
RS_SLOT = {19: [0], 20: [1, 2], 21: [3]}
RS_BANK = [0, 0, 1, 0]
RPV_SLOT = {21: [0, 1], 22: [2, 3]}
MIX_T = 22


def backwards(ap):
    *outer, (step, n) = [list(d) for d in ap.ap]
    return bass.AP(ap.tensor, ap.offset + (n - 1) * step, [*outer, [-step, n]])


def hybrid_layer(nc, xt, x, g_in, g_post_mix, g_pre_ffn, g_post_ffn, rel_bias,
                 w_in, w_out, w_gu, w_dn, ident_c, rope_c, decay_c, bucket_c, bias_row, out):
    with ExitStack() as ctx:
        def sb(name, shape, dt=F32, scope=ctx):
            return scope.enter_context(nc.sbuf_tensor(name, shape, dt))

        def sem(name):
            return ctx.enter_context(nc.semaphore(name))

        raw = sb("raw", [P, RAW, UNIT])
        w_hi = sb("w_hi", [P, RING, UNIT], F32R)
        w_lo = sb("w_lo", [P, RING, UNIT], F32R)
        a_hi = sb("a_hi", [P, NK, S], F32R)
        a_lo = sb("a_lo", [P, NK, S], F32R)
        m_hi = sb("m_hi", [P, NK, S], F32R)
        m_lo = sb("m_lo", [P, NK, S], F32R)
        xs = sb("xs", [P, NT, D])
        xg = sb("xg", [P, NT, D])
        gm = sb("gm", [P, D])
        gp = sb("gp", [P, D])
        gf = sb("gf", [P, D])
        junk = sb("junk", [P, CW])
        ident = sb("ident", [P, P])
        gin = sb("gin", [P, NK])
        ms = sb("ms", [P, 4, NT, 2])
        va = sb("va", [P, 4, NT])
        rstd = sb("rstd", [P, 4, NT])
        nq = sb("nq", [P, NT])
        half = sb("half", [P, RH])
        X_, MIX_, X1_, F_ = range(4)
        RET_ = 4
        FACTORS = [(what, t) for what in (X_, RET_, MIX_, X1_, F_) for t in range(NT)]

        with ExitStack() as attn:
            v = sb("v", [P, NT, CW], scope=attn)
            rv = sb("rv", [P, NT, CW], scope=attn)
            decay = sb("decay", [P, RH, 3 * P], scope=attn)
            rope = sb("rope", [P, NT, 3, RD // 2], scope=attn)
            lmin = sb("lmin", [P, NT, MH], scope=attn)
            esum = sb("esum", [P, NT, MH], scope=attn)
            erec = sb("erec", [P, NT, MH], scope=attn)
            rms4 = sb("rms4", [P, NT, RH], scope=attn)
            rs4 = sb("rs4", [P, NT, RH], scope=attn)
            with ExitStack() as early:
                xT = sb("xT", [P, NK, S], scope=early)
                qn = sb("qn", [P, NT, CW], scope=early)
                kn = sb("kn", [P, NT, CW], scope=early)
                rel = sb("rel", [BUCKETS + 1, MH], scope=early)
                bucket = sb("bucket", [BUCKETS + 1, REV], scope=early)
                brow = sb("brow", [MH, REV], scope=early)
            with ExitStack() as late:
                rot = sb("rot", [P, NT, CW], scope=late)
                rot_b = sb("rot_b", [P, CW], scope=late)
                rT = sb("rT", [P, 4, S], scope=late)
                rs = sb("rs", [P, RH, 3 * P], scope=late)
                with ExitStack() as mid:
                    bias = sb("bias", [P, MH, S], scope=mid)
                    qT = sb("qT", [P, MB, S], scope=mid)
                    kT = sb("kT", [P, MB, S], scope=mid)
                    pr = sb("pr", [P, 3, 3 * P], scope=mid)
                    pT = sb("pT", [P, 2, 3 * P], scope=mid)
                with ExitStack() as tail:
                    mix = sb("mix", [P, NT, D], scope=tail)
                    ret = sb("ret", [P, NT, CW], scope=tail)
                    gate = sb("gate", [P, NT, CW], scope=tail)
        with ExitStack() as ffn:
            d_hi = sb("d_hi", [P, DRING, UNIT], F32R, scope=ffn)
            d_lo = sb("d_lo", [P, DRING, UNIT], F32R, scope=ffn)
            h_hi = sb("h_hi", [P, NT, DN, P], F32R, scope=ffn)
            h_lo = sb("h_lo", [P, NT, DN, P], F32R, scope=ffn)
            sil = sb("sil", [P, NT, FG], scope=ffn)
            hid = sb("hid", [P, NT, FG], scope=ffn)
            res = sb("res", [P, NT, D], scope=ffn)

        bank01 = ctx.enter_context(nc.psum_tensor("bank01", [P, 2, CW], F32))
        bank23 = ctx.enter_context(nc.psum_tensor("bank23", [P, 2, CW], F32))
        bank45 = ctx.enter_context(nc.psum_tensor("bank45", [P, 2, CW], F32))
        bank67 = ctx.enter_context(nc.psum_tensor("bank67", [P, 2, CW], F32))
        pj = [bank01, bank23]
        wk = bank45
        po = bank67
        ro = bank01
        pm = [bank67, bank23]
        ph = bank45
        pg = bank01
        pt = bank45
        pf = [bank67, bank23]

        raw_loaded = [sem(f"raw_loaded{i}") for i in range(RAW)]
        hi_ready = sem("hi_ready")
        lo_ready = sem("lo_ready")
        w_used = sem("w_used")
        d_used = sem("d_used")
        xt_loaded = [sem(f"xt_loaded{i}") for i in range(NK // KPU)]
        gin_loaded = sem("gin_loaded")
        x_loaded = sem("x_loaded")
        gm_loaded = sem("gm_loaded")
        gp_loaded = sem("gp_loaded")
        gf_loaded = sem("gf_loaded")
        ident_loaded = sem("ident_loaded")
        rope_loaded = sem("rope_loaded")
        decay_loaded = sem("decay_loaded")
        rel_loaded = sem("rel_loaded")
        rel_one = sem("rel_one")
        brow_done = sem("brow_done")
        brow_ready = sem("brow_ready")
        brow_stored = sem("brow_stored")
        bias_loaded = sem("bias_loaded")
        x_hi = sem("x_hi")
        x_lo = sem("x_lo")
        sq_done = sem("sq_done")
        stat = sem("stat")
        var_ready = sem("var_ready")
        half_ready = sem("half_ready")
        rstd_ready = sem("rstd_ready")
        nq_ready = sem("nq_ready")
        proj_done = sem("proj_done")
        q_nat = sem("q_nat")
        k_nat = sem("k_nat")
        v_nat = sem("v_nat")
        rv_nat = sem("rv_nat")
        rot_ready = sem("rot_ready")
        gate_ready = sem("gate_ready")
        q_turned = sem("q_turned")
        k_turned = sem("k_turned")
        r_turned = sem("r_turned")
        qT_ready = sem("qT_ready")
        kT_ready = sem("kT_ready")
        rT_ready = sem("rT_ready")
        s_done = sem("s_done")
        l_ready = sem("l_ready")
        p_ready = sem("p_ready")
        pt_done = sem("pt_done")
        pT_ready = sem("pT_ready")
        pv_done = sem("pv_done")
        rs_done = sem("rs_done")
        rs_ready = sem("rs_ready")
        ro_done = sem("ro_done")
        sq4_done = sem("sq4_done")
        ret_ready = sem("ret_ready")
        mix_ready = sem("mix_ready")
        mix_turned = sem("mix_turned")
        mhi_ready = sem("mhi_ready")
        mlo_ready = sem("mlo_ready")
        wm_done = sem("wm_done")
        xg_ready = sem("xg_ready")
        hg_ready = sem("hg_ready")
        hg_turned = sem("hg_turned")
        ahi_ready = sem("ahi_ready")
        alo_ready = sem("alo_ready")
        x1_ready = sem("x1_ready")
        gu_done = sem("gu_done")
        sil_ready = [sem(f"sil_ready{t}") for t in range(NT)]
        hid_ready = [sem(f"hid_ready{t}") for t in range(NT)]
        h_turned = [sem(f"h_turned{t}") for t in range(NT)]
        hhi_ready = [sem(f"hhi_ready{t}") for t in range(NT)]
        hlo_ready = [sem(f"hlo_ready{t}") for t in range(NT)]
        dn_done = sem("dn_done")
        f_done = sem("f_done")
        res_part = sem("res_part")
        res_ready = sem("res_ready")
        out_stored = sem("out_stored")

        def gu_n(g, s):
            return N_IN + N_OUT + GU + PER * (g - 1) + s

        def dn_n(g, j):
            if isinstance(g, int) and g == NF - 1:
                return N_IN + N_OUT + GU + PER * g + j
            return N_IN + N_OUT + GU + PER * g + GU + j

        assert PER == RAW

        def wait_raw(eng, n, rounds=0):
            eng.wait_ge(raw_loaded[n % RAW], 16 * rounds + 16 * (n // RAW + 1))

        def wait_factor(eng, what, t):
            eng.wait_ge(rstd_ready, FACTORS.index((what, t)) + 1)

        def wait_projection(eng, group, t):
            if t == 0:
                eng.wait_ge(proj_done, group + 1)
            else:
                eng.wait_ge(w_used, UPG * (group + 1))

        def wait_mixer(eng, t, c):
            if (t, c) == (1, 1):
                eng.wait_ge(w_used, N_IN + N_OUT)
            else:
                eng.wait_ge(wm_done, 2 * t + c + 1)

        def wait_gate_up(eng, g, t):
            if t == 0:
                eng.wait_ge(gu_done, g + 1)
            else:
                eng.wait_ge(w_used, GU * g + (N_IN + N_OUT + GU))

        def wait_down(eng, g, t):
            if t == 0:
                eng.wait_ge(dn_done, g + 1)
            else:
                eng.wait_ge(d_used, DN * g + DN)

        block = ctx.enter_context(nc.Block())

        @block.sync
        def _(sp):
            def load(n, slot, src):
                if not (isinstance(n, int) and n < RAW):
                    sp.wait_ge(lo_ready, n - RAW + 1)
                sp.dma_start(raw[:, slot, :], src).then_inc(raw_loaded[slot], 16)

            for n in range(N_IN):
                load(n, n % RAW, w_in[n])
            for i in range(N_OUT):
                load(N_IN + i, (N_IN + i) % RAW, w_out[i])
            base = N_IN + N_OUT
            for s in range(GU):
                load(base + s, (base + s) % RAW, w_gu[s])

            def group(g, n0):
                for s in range(GU):
                    load(gu_n(g, s), (n0 + s) % RAW, w_gu[GU * g + s])
                for j in range(DN):
                    load(dn_n(g - 1, j), (n0 + GU + j) % RAW, w_dn[DN * (g - 1) + j])

            group(1, gu_n(1, 0))
            group(2, gu_n(2, 0))
            with sp.Fori(3, NF - 1, 2) as g:
                group(g, gu_n(3, 0))
                group(g + 1, gu_n(4, 0))
            for j in range(DN):
                load(dn_n(NF - 1, j), dn_n(NF - 1, j) % RAW, w_dn[DN * (NF - 1) + j])

            for t in range(NT):
                for c in range(2):
                    sp.wait_ge(res_ready, 2 * t + c + 1)
                    sp.dma_start(out[t * P:(t + 1) * P, c * CW:(c + 1) * CW],
                                 res[:, t, c * CW:(c + 1) * CW]).then_inc(out_stored, 16)
            sp.wait_ge(out_stored, 16 * 2 * NT)

        @block.gpsimd
        def _(pool):
            def factor(i):
                what, t = FACTORS[i]
                src = rms4[:, t, :] if what == RET_ else va[:, what, t:t + 1]
                dst = rs4[:, t, :] if what == RET_ else rstd[:, what, t:t + 1]
                pool.wait_ge(var_ready, i + 1)
                pool.tensor_tensor(dst, src, half[:, 0:src.shape[1]], ALU.pow).then_inc(rstd_ready, 1)

            pool.memset(rel[BUCKETS:BUCKETS + 1, :], 1.0).then_inc(rel_one, 1)
            pool.wait_ge(rel_one, 1)
            pool.memset(half[:, :], -0.5).then_inc(half_ready, 1)
            pool.wait_ge(half_ready, 1)
            pool.dma_start(rel[0:BUCKETS, :], rel_bias).then_inc(rel_loaded, 16)
            pool.dma_start(bucket[:, :], bucket_c).then_inc(rel_loaded, 16)
            pool.dma_start(ident[:, :], ident_c).then_inc(ident_loaded, 16)
            pool.dma_start(xs[:, :, :], x.rearrange("(t p) d -> p t d", p=P)).then_inc(x_loaded, 16)
            pool.dma_start(gm[:, :], g_post_mix.broadcast_to([P, D])).then_inc(gm_loaded, 16)
            pool.dma_start(gp[:, :], g_pre_ffn.broadcast_to([P, D])).then_inc(gp_loaded, 16)
            pool.wait_ge(brow_ready, 1)
            pool.dma_start(bias_row, brow[:, :]).then_inc(brow_stored, 16)
            pool.wait_ge(brow_stored, 16)
            pool.dma_start(bias[:, :, :], bass.AP(bias_row.tensor, 0, [[1, P], [REV, MH], [1, S]])
                           ).then_inc(bias_loaded, 16)
            pool.dma_start(rope[:, :, :, :], rope_c).then_inc(rope_loaded, 16)
            pool.dma_start(decay[:, :, :], decay_c).then_inc(decay_loaded, 16)
            pool.dma_start(gf[:, :], g_post_ffn.broadcast_to([P, D])).then_inc(gf_loaded, 16)
            for i in range(NT):
                factor(i)
            pool.wait_ge(x_loaded, 16)
            pool.wait_ge(gp_loaded, 16)
            pool.wait_ge(gm_loaded, 16)
            for t in range(NT):
                pool.tensor_tensor(xg[:, t, :], xs[:, t, :], gp[:, :], ALU.mult).then_inc(xg_ready, 1)
            pool.wait_ge(xg_ready, NT)
            pool.tensor_tensor(gp[:, :], gm[:, :], gp[:, :], ALU.mult).then_inc(xg_ready, 1)
            for i in range(NT, len(FACTORS)):
                factor(i)

        @block.scalar
        def _(act):
            def hi_in(n):
                wait_raw(act, n)
                if n >= RING:
                    act.wait_ge(w_used, n - RING + 1)
                act.activation(w_hi[:, n % RING, :], raw[:, n % RAW, :], ACT.Copy).then_inc(hi_ready, 1)

            squared = [0]

            def squares(what, t, c, src):
                if squared[0]:
                    act.wait_ge(sq_done, squared[0])
                squared[0] += 1
                act.activation(junk[:, 0:CW], src, ACT.Square, scale=1.0 / math.sqrt(D),
                               accum_out=ms[:, what, t, c:c + 1]).then_inc(sq_done, 1)

            for i in range(NK // KPU):
                act.dma_start(xT[:, KPU * i:KPU * (i + 1), :], xt[:, KPU * i:KPU * (i + 1), :]
                              ).then_inc(xt_loaded[i], 16)
                if i == 0:
                    act.dma_start(gin[:, :], g_in).then_inc(gin_loaded, 16)
            act.wait_ge(gin_loaded, 16)
            for i in range(NK // KPU):
                act.wait_ge(xt_loaded[i], 16)
                for k in range(KPU * i, KPU * (i + 1)):
                    act.activation(a_hi[:, k, :], xT[:, k, :], ACT.Copy, scale=gin[:, k:k + 1]
                                   ).then_inc(x_hi, 1)
                hi_in(i)
            act.wait_ge(brow_done, 1)
            act.activation(brow[:, :], wk[0:MH, 0, 0:REV], ACT.Copy).then_inc(brow_ready, 1)
            hi_in(4)
            act.wait_ge(x_loaded, 16)
            for t in range(NT):
                for c in range(2):
                    squares(X_, t, c, xs[:, t, c * CW:(c + 1) * CW])

            def rows_out(dst, group, scale, done):
                for t in range(NT):
                    wait_projection(act, group, t)
                    act.activation(dst[:, t, :], pj[group % 2][:, t, :], ACT.Copy,
                                   scale=scale(t)).then_inc(done, 1)

            def turned_out(dst, src, turned, done, order=lambda ap: ap):
                for t in range(NT):
                    act.wait_ge(turned, t + 1)
                    act.activation(dst[:, :, t * P:(t + 1) * P],
                                   order(src[:, t, :].rearrange("p (b i) -> p b i", i=P)), ACT.Copy
                                   ).then_inc(done, 1)

            def r_x(t):
                return rstd[:, X_, t:t + 1]

            for u in range(N_IN):
                hi_in(u + LEAD)
                if u == UPG:
                    act.wait_ge(nq_ready, 1)
                    wait_factor(act, X_, NT - 1)
                    rows_out(qn, 0, lambda t: nq[:, t:t + 1], q_nat)
                if u == Q_T + 1:
                    turned_out(qT, wk, q_turned, qT_ready, order=backwards)
                if u == 2 * UPG:
                    rows_out(kn, 1, r_x, k_nat)
                if u == K_T + 1:
                    turned_out(kT, wk, k_turned, kT_ready)
                if u == 3 * UPG:
                    rows_out(v, 2, r_x, v_nat)
                if 0 <= u - (S0 + 1) < MH:
                    h = u - (S0 + 1)
                    act.wait_ge(l_ready, h + 1)
                    for t, (a, b) in enumerate([(0, P), (P, 3 * P)]):
                        act.activation(pr[:, h % 3, a:b], pr[:, h % 3, a:b], ACT.Exp,
                                       bias=lmin[:, t, h:h + 1], scale=-1.0,
                                       accum_out=esum[:, t, h:h + 1]).then_inc(p_ready, 1)
                if u == RQK_T + 1:
                    turned_out(rT, bank23, r_turned, rT_ready)
                if u == 5 * UPG:
                    rows_out(rv, 4, r_x, rv_nat)
                if u == MIX_T + 1:
                    for t, b in ((0, 1), (1, 0)):
                        act.wait_ge(mix_turned, t + 1)
                        act.activation(m_hi[:, 4:8, t * P:(t + 1) * P],
                                       backwards(wk[:, b, :].rearrange("p (b i) -> p b i", i=P)), ACT.Copy
                                       ).then_inc(mhi_ready, 1)
                    act.wait_ge(ro_done, RH)
                    for t in range(NT):
                        act.activation(ret[:, t, :], ro[:, t, :], ACT.Square, scale=1.0 / math.sqrt(RV)
                                       ).then_inc(sq4_done, 1)
            for t in range(NT):
                wait_projection(act, NG - 1, t)
                act.activation(gate[:, t, :], pj[1][:, t, :], ACT.Silu, scale=r_x(t)).then_inc(gate_ready, 1)
            for n in range(N_IN + LEAD, N_IN + N_OUT):
                hi_in(n)
            for t, b in ((0, 1), (1, 0)):
                act.wait_ge(mix_turned, NT + t + 1)
                act.activation(m_hi[:, 0:4, t * P:(t + 1) * P],
                               wk[:, b, :].rearrange("p (b i) -> p b i", i=P), ACT.Copy
                               ).then_inc(mhi_ready, 1)
            for s in range(GU):
                hi_in(N_IN + N_OUT + s)
            for t in range(NT):
                for c in range(2):
                    wait_mixer(act, t, c)
                    squares(MIX_, t, c, pm[t][:, c, :])
                for c in range(2):
                    act.wait_ge(hg_turned, 2 * t + c + 1)
                    act.activation(a_hi[:, 4 * c:4 * c + 4, t * P:(t + 1) * P],
                                   ph[:, c, :].rearrange("p (b i) -> p b i", i=P), ACT.Copy
                                   ).then_inc(ahi_ready, 1)
                if t == 0:
                    act.wait_ge(x1_ready, 1)
                    for c in range(2):
                        squares(X1_, 0, c, xs[:, 0, c * CW:(c + 1) * CW])
            act.wait_ge(x1_ready, 2)
            for c in range(2):
                squares(X1_, 1, c, xs[:, 1, c * CW:(c + 1) * CW])

            def hi_gu(g, s, g0):
                n0 = gu_n(g0, s)
                wait_raw(act, n0, g - g0)
                a0 = N_IN + N_OUT + GU * g0 + s
                act.wait_ge(w_used, N_IN + N_OUT + GU * g + s - RING + 1)
                act.activation(w_hi[:, a0 % RING, :], raw[:, n0 % RAW, :], ACT.Copy).then_inc(hi_ready, 1)

            def hi_dn(g, j, g0):
                n0 = dn_n(g0, j)
                wait_raw(act, n0, g - g0)
                if not (isinstance(g, int) and DN * g + j < DRING):
                    act.wait_ge(d_used, DN * g + j - DRING + 1)
                act.activation(d_hi[:, (DN * g0 + j) % DRING, :], raw[:, n0 % RAW, :], ACT.Copy
                               ).then_inc(hi_ready, 1)

            def silu(g, t):
                wait_gate_up(act, g, t)
                if not (isinstance(g, int) and g == 0):
                    act.wait_ge(hid_ready[t], g)
                act.activation(sil[:, t, :], pg[:, t, 0:FG], ACT.Silu, scale=rstd[:, X1_, t:t + 1]
                               ).then_inc(sil_ready[t], 1)

            def h_hi_part(g, t):
                act.wait_ge(h_turned[t], g + 1)
                if not (isinstance(g, int) and g == 0):
                    wait_down(act, g - 1, t)
                act.activation(h_hi[:, t, :, :], pt[:, t, 0:FG].rearrange("p (b i) -> p b i", i=P),
                               ACT.Copy).then_inc(hhi_ready[t], 1)

            def group(g, g0, more=True):
                if more:
                    for s in range(GU - 1):
                        hi_gu(g + 1, s, g0 + 1)
                if g0 == 0:
                    wait_factor(act, X1_, 0)
                silu(g, 0)
                if g0 > 0:
                    h_hi_part(g - 1, 1)
                if more:
                    hi_gu(g + 1, GU - 1, g0 + 1)
                for j in range(DN):
                    hi_dn(g, j, g0)
                if g0 == 0:
                    wait_factor(act, X1_, 1)
                silu(g, 1)
                h_hi_part(g, 0)

            group(0, 0)
            group(1, 1)
            with act.Fori(2, NF - 2, 2) as g:
                group(g, 2)
                group(g + 1, 3)
            group(NF - 1, NF - 1, more=False)
            h_hi_part(NF - 1, 1)
            for t in range(NT):
                for c in range(2):
                    act.wait_ge(f_done, 2 * t + c + 1)
                    squares(F_, t, c, pf[t][:, c, :])

        @block.vector
        def _(dve):
            steps = [0]

            def small(ins):
                steps[0] += 1
                ins.then_inc(stat, 1)
                dve.wait_ge(stat, steps[0])

            def lo_in(n):
                dve.wait_ge(hi_ready, n + 1)
                dve.tensor_tensor(w_lo[:, n % RING, :], raw[:, n % RAW, :],
                                  w_hi[:, n % RING, :].bitcast(F32), ALU.subtract).then_inc(lo_ready, 1)

            def factor(what, t, squared):
                dve.wait_ge(sq_done, squared)
                dve.tensor_scalar(va[:, what, t:t + 1], ms[:, what, t, 0:1], ms[:, what, t, 1:2], EPS,
                                  ALU.add, ALU.add).then_inc(var_ready, 1)

            dve.wait_ge(gin_loaded, 16)
            for i in range(NK // KPU):
                dve.wait_ge(xt_loaded[i], 16)
                for k in range(KPU * i, KPU * (i + 1)):
                    dve.wait_ge(x_hi, k + 1)
                    dve.scalar_tensor_tensor(out=a_lo[:, k, :], in0=xT[:, k, :], scalar=gin[:, k:k + 1],
                                             in1=a_hi[:, k, :].bitcast(F32), op0=ALU.mult,
                                             op1=ALU.subtract).then_inc(x_lo, 1)
                lo_in(i)
            lo_in(4)
            for t in range(NT):
                factor(X_, t, 2 * t + 2)
            wait_factor(dve, X_, NT - 1)
            dve.tensor_scalar(nq[:, :], rstd[:, X_, :], -1.0 / math.sqrt(MD), None, ALU.mult
                              ).then_inc(nq_ready, 1)

            def rotary(t):
                half = RD // 2
                r = rstd[:, X_, t:t + 1]
                src = pj[1][:, t, :].rearrange("p (n d) -> p n d", d=half)
                halves = pj[1][:, t, :].rearrange("p (n a d) -> p n a d", a=2, d=half)
                turned = rot_b[:, :].rearrange("p (n a d) -> p n a d", a=2, d=half)

                def table(i, n):
                    return rope[:, t, i:i + 1, :].broadcast_to([P, n, half])

                wait_projection(dve, 3, t)
                dve.scalar_tensor_tensor(out=rot[:, t, :].rearrange("p (n d) -> p n d", d=half), in0=src,
                                         scalar=r, in1=table(0, 4 * RH), op0=ALU.mult, op1=ALU.mult)
                dve.scalar_tensor_tensor(out=turned[:, :, 0, :], in0=halves[:, :, 1, :], scalar=r,
                                         in1=table(2, 2 * RH), op0=ALU.mult, op1=ALU.mult)
                small(dve.scalar_tensor_tensor(out=turned[:, :, 1, :], in0=halves[:, :, 0, :], scalar=r,
                                               in1=table(1, 2 * RH), op0=ALU.mult, op1=ALU.mult))
                dve.tensor_tensor(rot[:, t, :], rot[:, t, :], rot_b[:, :], ALU.add).then_inc(rot_ready, 1)
                dve.wait_ge(rot_ready, t + 1)

            def logits(h):
                dve.wait_ge(s_done, h + 1)
                if h >= 3:
                    dve.wait_ge(pt_done, h - 2)
                for t, (a, b) in enumerate([(0, P), (P, 3 * P)]):
                    ins = dve.tensor_tensor_reduce(out=pr[:, h % 3, a:b], in0=wk[:, 0, a:b],
                                                   in1=bias[:, h, P - t * P:S], scale=1.0,
                                                   scalar=3.0e38, op0=ALU.add, op1=ALU.min,
                                                   accum_out=lmin[:, t, h:h + 1])
                ins.then_inc(l_ready, 1)

            for u in range(N_IN):
                lo_in(u + LEAD)
                if u == 4 * UPG:
                    dve.wait_ge(rope_loaded, 16)
                    rotary(0)
                if u == 4 * UPG + 1:
                    rotary(1)
                if 0 <= u - (S0 + 1) < MH:
                    if u == S0 + 1:
                        dve.wait_ge(bias_loaded, 16)
                    logits(u - (S0 + 1))
                if 0 <= u - (S0 + PT_LAG + 1) < MH:
                    h = u - (S0 + PT_LAG + 1)
                    dve.wait_ge(pt_done, h + 1)
                    if h >= 2:
                        dve.wait_ge(pv_done, h - 1)
                    dve.tensor_copy(pT[:, h % 2, :], wk[:, 1, 0:3 * P]).then_inc(pT_ready, 1)
                for h in RS_SLOT.get(u - 1, []):
                    if h == 0:
                        dve.wait_ge(decay_loaded, 16)
                    dve.wait_ge(rs_done, h + 1)
                    dve.tensor_tensor(rs[:, h, :], wk[:, RS_BANK[h], 0:3 * P], decay[:, h, :], ALU.mult
                                      ).then_inc(rs_ready, 1)
                if u == S0 + PV_LAG + MH:
                    dve.wait_ge(p_ready, NT * MH)
                    small(dve.reciprocal(erec[:, :, :], esum[:, :, :]))
                    dve.wait_ge(pv_done, MH)
                    for t in range(NT):
                        dve.tensor_tensor(mix[:, t, CW:D].rearrange("p (h e) -> p h e", e=MD),
                                          po[:, t, :].rearrange("p (h e) -> p h e", e=MD),
                                          erec[:, t, :].unsqueeze(2).broadcast_to([P, MH, MD]),
                                          ALU.mult).then_inc(mix_ready, 1)
                if u == MIX_T + 1:
                    for t, b in ((0, 1), (1, 0)):
                        dve.wait_ge(mhi_ready, t + 1)
                        dve.tensor_tensor(m_lo[:, 4:8, t * P:(t + 1) * P],
                                          backwards(wk[:, b, :].rearrange("p (b i) -> p b i", i=P)),
                                          m_hi[:, 4:8, t * P:(t + 1) * P].bitcast(F32), ALU.subtract
                                          ).then_inc(mlo_ready, 1)
                    for t in range(NT):
                        dve.wait_ge(sq4_done, t + 1)
                        small(dve.tensor_reduce(rms4[:, t, :],
                                                ret[:, t, :].rearrange("p (h e) -> p h e", e=RV),
                                                AX_X, ALU.add))
                        dve.tensor_scalar(rms4[:, t, :], rms4[:, t, :], EPS, None, ALU.add
                                          ).then_inc(var_ready, 1)
                    for t in range(NT):
                        wait_factor(dve, RET_, t)
                        dve.tensor_tensor(ret[:, t, :].rearrange("p (h e) -> p h e", e=RV),
                                          ro[:, t, :].rearrange("p (h e) -> p h e", e=RV),
                                          rs4[:, t, :].unsqueeze(2).broadcast_to([P, RH, RV]),
                                          ALU.mult).then_inc(ret_ready, 1)
            for t in range(NT):
                dve.wait_ge(gate_ready, t + 1)
                dve.wait_ge(ret_ready, t + 1)
                dve.tensor_tensor(mix[:, t, 0:CW], ret[:, t, :], gate[:, t, :], ALU.mult
                                  ).then_inc(mix_ready, 1)
            for n in range(N_IN + LEAD, N_IN + N_OUT):
                lo_in(n)
            for t, b in ((0, 1), (1, 0)):
                dve.wait_ge(mhi_ready, NT + t + 1)
                dve.tensor_tensor(m_lo[:, 0:4, t * P:(t + 1) * P],
                                  wk[:, b, :].rearrange("p (b i) -> p b i", i=P),
                                  m_hi[:, 0:4, t * P:(t + 1) * P].bitcast(F32), ALU.subtract
                                  ).then_inc(mlo_ready, 1)
            for s in range(GU):
                lo_in(N_IN + N_OUT + s)

            def scaled(t):
                factor(MIX_, t, 10 if t else 6)
                if t == 0:
                    dve.wait_ge(xg_ready, NT + 1)
                wait_factor(dve, MIX_, t)
                for c in range(2):
                    cols = slice(c * CW, (c + 1) * CW)
                    small(dve.scalar_tensor_tensor(out=mix[:, t, cols], in0=pm[t][:, c, :],
                                                   scalar=rstd[:, MIX_, t:t + 1], in1=gp[:, cols],
                                                   op0=ALU.mult, op1=ALU.mult))
                    dve.tensor_tensor(xg[:, t, cols], mix[:, t, cols], xg[:, t, cols], ALU.add
                                      ).then_inc(hg_ready, 1)

            def a_lo_part(t, c):
                dve.wait_ge(ahi_ready, 2 * t + c + 1)
                dve.tensor_tensor(a_lo[:, 4 * c:4 * c + 4, t * P:(t + 1) * P],
                                  ph[:, c, :].rearrange("p (b i) -> p b i", i=P),
                                  a_hi[:, 4 * c:4 * c + 4, t * P:(t + 1) * P].bitcast(F32), ALU.subtract
                                  ).then_inc(alo_ready, 1)

            def residual(t):
                small(dve.scalar_tensor_tensor(out=mix[:, t, :].rearrange("p (c d) -> p c d", c=2),
                                               in0=pm[t][:, :, :],
                                               scalar=rstd[:, MIX_, t:t + 1],
                                               in1=gm[:, :].rearrange("p (c d) -> p c d", c=2),
                                               op0=ALU.mult, op1=ALU.mult))
                dve.tensor_tensor(xs[:, t, :], xs[:, t, :], mix[:, t, :], ALU.add).then_inc(x1_ready, 1)

            dve.wait_ge(gm_loaded, 16)
            scaled(0)
            a_lo_part(0, 0)
            a_lo_part(0, 1)
            residual(0)
            scaled(1)
            a_lo_part(1, 0)
            a_lo_part(1, 1)
            residual(1)
            factor(X1_, 0, 8)
            factor(X1_, 1, 12)

            def lo_gu(g, s, g0):
                n0 = gu_n(g0, s)
                slot = (N_IN + N_OUT + GU * g0 + s) % RING
                dve.wait_ge(hi_ready, gu_n(g, s) + 1)
                dve.tensor_tensor(w_lo[:, slot, :], raw[:, n0 % RAW, :], w_hi[:, slot, :].bitcast(F32),
                                  ALU.subtract).then_inc(lo_ready, 1)

            def lo_dn(g, j, g0):
                n0 = dn_n(g0, j)
                slot = (DN * g0 + j) % DRING
                dve.wait_ge(hi_ready, dn_n(g, j) + 1)
                dve.tensor_tensor(d_lo[:, slot, :], raw[:, n0 % RAW, :], d_hi[:, slot, :].bitcast(F32),
                                  ALU.subtract).then_inc(lo_ready, 1)

            def hidden(g, t):
                dve.wait_ge(sil_ready[t], g + 1)
                if not (isinstance(g, int) and g == 0):
                    dve.wait_ge(h_turned[t], g)
                dve.scalar_tensor_tensor(out=hid[:, t, :], in0=pg[:, t, FG:2 * FG],
                                         scalar=rstd[:, X1_, t:t + 1], in1=sil[:, t, :],
                                         op0=ALU.mult, op1=ALU.mult).then_inc(hid_ready[t], 1)

            def h_lo_part(g, t):
                dve.wait_ge(hhi_ready[t], g + 1)
                dve.tensor_tensor(h_lo[:, t, :, :], pt[:, t, 0:FG].rearrange("p (b i) -> p b i", i=P),
                                  h_hi[:, t, :, :].bitcast(F32), ALU.subtract).then_inc(hlo_ready[t], 1)

            def group(g, g0, more=True):
                if more:
                    for s in range(GU - 1):
                        lo_gu(g + 1, s, g0 + 1)
                hidden(g, 0)
                if g0 > 0:
                    h_lo_part(g - 1, 1)
                if more:
                    lo_gu(g + 1, GU - 1, g0 + 1)
                for j in range(DN):
                    lo_dn(g, j, g0)
                hidden(g, 1)
                h_lo_part(g, 0)

            group(0, 0)
            group(1, 1)
            with dve.Fori(2, NF - 2, 2) as g:
                group(g, 2)
                group(g + 1, 3)
            group(NF - 1, NF - 1, more=False)
            h_lo_part(NF - 1, 1)
            dve.wait_ge(gf_loaded, 16)
            for t in range(NT):
                factor(F_, t, 12 + 2 * t + 2)
                wait_factor(dve, F_, t)
                for c in range(2):
                    cols = slice(c * CW, (c + 1) * CW)
                    dve.scalar_tensor_tensor(out=res[:, t, cols], in0=pf[t][:, c, :],
                                             scalar=rstd[:, F_, t:t + 1], in1=gf[:, cols],
                                             op0=ALU.mult, op1=ALU.mult).then_inc(res_part, 1)
                    dve.wait_ge(res_part, 2 * t + c + 1)
                    dve.tensor_tensor(res[:, t, cols], res[:, t, cols], xs[:, t, cols], ALU.add
                                      ).then_inc(res_ready, 1)

        @block.tensor
        def _(pe):
            def product(acc, hi, lo, wh, wl, first, last):
                pe.matmul(acc, hi, wh, start=first, stop=False)
                pe.matmul(acc, hi, wl, start=False, stop=False)
                return pe.matmul(acc, lo, wh, start=False, stop=last)

            def tile(t):
                return slice(t * P, (t + 1) * P)

            def turn(dst, src, blocks, done):
                for b in range(blocks):
                    ins = pe.transpose(dst[:, b * P:(b + 1) * P], src[:, b * P:(b + 1) * P], ident[:, :])
                ins.then_inc(done, 1)

            def head_rows(h):
                return slice(64 * (h % 2), 64 * (h % 2) + 64)

            pe.wait_ge(rel_one, 1)
            pe.wait_ge(rel_loaded, 32)
            pe.matmul(wk[0:MH, 0, 0:REV], rel[:, :], bucket[:, :], start=True, stop=True).then_inc(brow_done, 1)

            for u in range(N_IN):
                g, s = divmod(u, UPG)
                pe.wait_ge(lo_ready, u + 1)
                for t in range(NT):
                    if s == 0:
                        if g == 2:
                            pe.wait_ge(q_nat, t + 1)
                        if g == 3:
                            pe.wait_ge(k_nat, t + 1)
                        if g == 4:
                            pe.wait_ge(v_nat, t + 1)
                        if g == 5:
                            pe.wait_ge(rT_ready, t + 1)
                    for i in range(KPU):
                        k = KPU * s + i
                        if g == 0 and t == 0:
                            pe.wait_ge(x_lo, k + 1)
                        ins = product(pj[g % 2][:, t, :], a_hi[:, k, tile(t)], a_lo[:, k, tile(t)],
                                      w_hi[:, u % RING, i * CW:(i + 1) * CW],
                                      w_lo[:, u % RING, i * CW:(i + 1) * CW],
                                      first=(k == 0), last=(k == NK - 1))
                    if s == UPG - 1 and t == 0:
                        ins.then_inc(proj_done, 1)
                ins.then_inc(w_used, 1)

                if u == Q_T:
                    pe.wait_ge(ident_loaded, 16)
                    pe.wait_ge(brow_ready, 1)
                    for t in range(NT):
                        pe.wait_ge(q_nat, t + 1)
                        turn(wk[:, t, :], qn[:, t, :], MB, q_turned)
                if u == K_T:
                    for t in range(NT):
                        pe.wait_ge(k_nat, t + 1)
                        pe.wait_ge(qT_ready, t + 1)
                        turn(wk[:, t, :], kn[:, t, :], MB, k_turned)
                if 0 <= u - S0 < MH:
                    h = u - S0
                    rows, b = head_rows(h), h // 2
                    if h == 0:
                        pe.wait_ge(kT_ready, NT)
                    else:
                        pe.wait_ge(l_ready, h)
                    pe.matmul(wk[:, 0, 0:P], qT[rows, b, tile(0)], kT[rows, b, tile(0)],
                              start=True, stop=True)
                    pe.matmul(wk[:, 0, P:3 * P], qT[rows, b, tile(1)], kT[rows, b, :],
                              start=True, stop=True).then_inc(s_done, 1)
                if 0 <= u - (S0 + PT_LAG) < MH:
                    h = u - (S0 + PT_LAG)
                    pe.wait_ge(p_ready, NT * (h + 1))
                    if h > 0:
                        pe.wait_ge(pT_ready, h)
                    turn(wk[:, 1, :], pr[:, h % 3, :], 3, pt_done)
                if 0 <= u - (S0 + PV_LAG) < MH:
                    h = u - (S0 + PV_LAG)
                    cols = slice(h * MD, (h + 1) * MD)
                    pe.wait_ge(pT_ready, h + 1)
                    if h == 0:
                        pe.wait_ge(v_nat, NT)
                    pe.matmul(po[:, 0, cols], pT[:, h % 2, 0:P], v[:, 0, cols], start=True, stop=True)
                    pe.matmul(po[:, 1, cols], pT[:, h % 2, P:2 * P], v[:, 0, cols], start=True, stop=False)
                    pe.matmul(po[:, 1, cols], pT[:, h % 2, 2 * P:3 * P], v[:, 1, cols],
                              start=False, stop=True).then_inc(pv_done, 1)
                if u == RQK_T:
                    for t in range(NT):
                        pe.wait_ge(rot_ready, t + 1)
                        turn(bank23[:, t, :], rot[:, t, :], 4, r_turned)
                for h in RS_SLOT.get(u, []):
                    rows, b = head_rows(h), h // 2
                    if h == 0:
                        pe.wait_ge(rT_ready, NT)
                        pe.wait_ge(l_ready, MH)
                    elif h == 2:
                        pe.wait_ge(pT_ready, MH)
                    else:
                        pe.wait_ge(rs_ready, 1 if h == 1 else 2)
                    pe.matmul(wk[:, RS_BANK[h], 0:2 * P], rT[rows, 2 + b, tile(0)], rT[rows, b, :],
                              start=True, stop=True)
                    pe.matmul(wk[:, RS_BANK[h], 2 * P:3 * P], rT[rows, 2 + b, tile(1)],
                              rT[rows, b, tile(1)], start=True, stop=True).then_inc(rs_done, 1)
                for h in RPV_SLOT.get(u, []):
                    cols = slice(h * RV, (h + 1) * RV)
                    if h == 0:
                        pe.wait_ge(rv_nat, NT)
                    pe.wait_ge(rs_ready, h + 1)
                    pe.matmul(ro[:, 0, cols], rs[:, h, 0:P], rv[:, 0, cols], start=True, stop=True)
                    pe.matmul(ro[:, 1, cols], rs[:, h, P:2 * P], rv[:, 0, cols], start=True, stop=False)
                    pe.matmul(ro[:, 1, cols], rs[:, h, 2 * P:3 * P], rv[:, 1, cols],
                              start=False, stop=True).then_inc(ro_done, 1)
                if u == MIX_T:
                    for t, b in ((0, 1), (1, 0)):
                        pe.wait_ge(mix_ready, t + 1)
                        pe.wait_ge(rs_ready, 3 if b else 4)
                        turn(wk[:, b, :], mix[:, t, CW:D], 4, mix_turned)

            def mixer(t, part, c):
                for i in range(4 * part, 4 * part + 4):
                    k, n = WOUT_K[i], N_IN + i
                    if t == 0:
                        pe.wait_ge(lo_ready, n + 1)
                    ins = product(pm[t][:, c, :], m_hi[:, k, tile(t)], m_lo[:, k, tile(t)],
                                  w_hi[:, n % RING, c * CW:(c + 1) * CW],
                                  w_lo[:, n % RING, c * CW:(c + 1) * CW],
                                  first=(i == 0), last=(i == N_OUT - 1))
                    if t == 1 and c == 1:
                        ins.then_inc(w_used, 1)
                return ins

            for t, b in ((0, 1), (1, 0)):
                pe.wait_ge(mlo_ready, t + 1)
                if t == 1:
                    pe.wait_ge(gate_ready, NT)
                for c in range(2):
                    mixer(t, 0, c)
                pe.wait_ge(mix_ready, NT + t + 1)
                pe.wait_ge(mlo_ready, t + 1)
                turn(wk[:, b, :], mix[:, t, 0:CW], 4, mix_turned)
            pe.wait_ge(mlo_ready, NT + 1)
            for c in range(2):
                mixer(0, 1, c).then_inc(wm_done, 1)
            pe.wait_ge(mlo_ready, 2 * NT)

            def turn_scaled(t, c):
                pe.wait_ge(hg_ready, 2 * t + c + 1)
                if t == 1:
                    pe.wait_ge(alo_ready, c + 1)
                turn(ph[:, c, :], xg[:, t, c * CW:(c + 1) * CW], 4, hg_turned)

            mixer(1, 1, 0).then_inc(wm_done, 1)
            turn_scaled(0, 0)
            mixer(1, 1, 1)
            turn_scaled(0, 1)

            def gate_up(g, t, g0, hook=None):
                if not (isinstance(g, int) and g == 0):
                    pe.wait_ge(hid_ready[t], g)
                for s in range(GU):
                    a0 = N_IN + N_OUT + GU * g0 + s
                    if t == 0:
                        pe.wait_ge(lo_ready, (gu_n(g, s) if g0 else N_IN + N_OUT + s) + 1)
                    for i in range(KPU):
                        k = KPU * s + i
                        if g0 == 0 and k % 4 == 0:
                            pe.wait_ge(alo_ready, 2 * t + k // 4 + 1)
                        ins = product(pg[:, t, :], a_hi[:, k, tile(t)], a_lo[:, k, tile(t)],
                                      w_hi[:, a0 % RING, i * CW:(i + 1) * CW],
                                      w_lo[:, a0 % RING, i * CW:(i + 1) * CW],
                                      first=(k == 0), last=(k == NK - 1))
                    if t == 1:
                        ins.then_inc(w_used, 1)
                    elif s == GU - 1:
                        ins.then_inc(gu_done, 1)
                    if hook:
                        hook(s)

            def turn_hidden(g, t):
                pe.wait_ge(hid_ready[t], g + 1)
                if not (isinstance(g, int) and g == 0):
                    pe.wait_ge(hlo_ready[t], g)
                turn(pt[:, t, :], hid[:, t, :], DN, h_turned[t])

            def down(g, t, g0, last=False):
                pe.wait_ge(hlo_ready[t], g + 1)
                if g0 == 0:
                    pe.wait_ge(x1_ready, t + 1)
                for c in range(2):
                    for j in range(DN):
                        slot = (DN * g0 + j) % DRING
                        if t == 0 and c == 0:
                            pe.wait_ge(lo_ready, dn_n(g, j) + 1)
                        ins = product(pf[t][:, c, :], h_hi[:, t, j, :], h_lo[:, t, j, :],
                                      d_hi[:, slot, c * CW:(c + 1) * CW],
                                      d_lo[:, slot, c * CW:(c + 1) * CW],
                                      first=(g0 == 0 and j == 0), last=(last and j == DN - 1))
                        if t == 1 and c == 1 and not last:
                            ins.then_inc(d_used, 1)
                    if last:
                        ins.then_inc(f_done, 1)
                if t == 0 and not last:
                    ins.then_inc(dn_done, 1)

            def group(g, g0):
                gate_up(g, 0, g0)
                turn_hidden(g - 1, 1)
                down(g - 1, 0, g0 - 1)
                gate_up(g, 1, g0)
                turn_hidden(g, 0)
                down(g - 1, 1, g0 - 1)

            def scaled_hook(s):
                if s >= 2:
                    turn_scaled(1, s - 2)

            gate_up(0, 0, 0, hook=scaled_hook)
            gate_up(0, 1, 0)
            turn_hidden(0, 0)
            group(1, 1)
            with pe.Fori(2, NF - 2, 2) as g:
                group(g, 2)
                group(g + 1, 3)
            group(NF - 1, NF - 1)
            turn_hidden(NF - 1, 1)
            down(NF - 1, 0, NF - 1, last=True)
            down(NF - 1, 1, NF - 1, last=True)


def _bucket(n):
    exact = BUCKETS // 2
    far = exact + (np.log(np.maximum(n, 1).astype(np.float32) / np.float32(exact))
                   / np.float32(math.log(MAX_DIST / exact)) * np.float32(BUCKETS - exact)).astype(np.int32)
    return np.where(n < exact, n, np.minimum(far, BUCKETS - 1))


def _constants():
    ident = np.eye(P, dtype=np.float32)
    half = RD // 2
    inv = np.float32(10000.0) ** (-np.arange(half, dtype=np.float32) / np.float32(half))
    ang = (np.arange(S, dtype=np.float32)[:, None] * inv[None, :]).astype(np.float32).astype(np.float64)
    rope = np.stack([np.cos(ang), np.sin(ang), -np.sin(ang)], 1).astype(np.float32)
    rope = np.ascontiguousarray(rope.reshape(NT, P, 3, half).transpose(1, 0, 2, 3))
    log_gamma = np.log1p(-np.exp(np.linspace(math.log(1.0 / 32), math.log(1.0 / 512), RH)))
    j = np.arange(P)[:, None]
    dist = np.concatenate([np.arange(S)[None, :] - j, np.arange(P)[None, :] - j], 1)
    decay = np.where(dist >= 0, np.exp(np.maximum(dist, 0)[None] * log_gamma[:, None, None]), 0.0) * RD ** -0.5
    decay = np.ascontiguousarray(decay.transpose(1, 0, 2)).astype(np.float32)
    n = S - 1 - np.arange(REV)
    bucket = np.zeros((BUCKETS + 1, REV), np.float32)
    past = n >= 0
    bucket[_bucket(np.maximum(n, 0))[past], np.arange(REV)[past]] = -1.0
    bucket[BUCKETS, ~past] = MASKED
    return {"ident_c": ident, "rope_c": rope, "decay_c": decay, "bucket_c": bucket}


def _laid_out(i):
    def a(name):
        return np.asarray(i[name])

    x = a("x")[0]
    w_in = a("w_in")[0].reshape(UPG, KPU, P, NG, CW)[:, :, :, ORDER]
    gate = a("w_gate")[0].reshape(GU, KPU, P, NF, FG)
    up = a("w_up")[0].reshape(GU, KPU, P, NF, FG)
    return {
        "xt": x.T.reshape(NK, P, S).transpose(1, 0, 2),
        "x": x,
        "g_in": a("pre_mix_norm")[0].reshape(NK, P).T,
        "g_post_mix": a("post_mix_norm"),
        "g_pre_ffn": a("pre_ffn_norm"),
        "g_post_ffn": a("post_ffn_norm"),
        "rel_bias": a("rel_bias"),
        "w_in": w_in.transpose(3, 0, 2, 1, 4).reshape(N_IN, P, UNIT),
        "w_out": a("w_out")[0].reshape(NK, P, D)[WOUT_K],
        "w_gu": np.stack([gate, up], 4).transpose(3, 0, 2, 1, 4, 5).reshape(NF * GU, P, UNIT),
        "w_dn": a("w_down")[0].reshape(NF * DN, P, D),
    }


def kernel(**inputs):
    import concourse.bacc as bacc
    from concourse.bass_utils import run_bass_kernel_spmd

    arrays = {k: np.ascontiguousarray(v) for k, v in {**_laid_out(inputs), **_constants()}.items()}
    nc = bacc.Bacc("TRN2", target_bir_lowering=False, num_devices=1)
    args = {k: nc.dram_tensor(f"in_{k}", v.shape, mybir.dt.from_np(v.dtype), kind="ExternalInput").ap()
            for k, v in arrays.items()}
    args["bias_row"] = nc.dram_tensor("bias_row", (MH, REV), F32, kind="Internal").ap()
    args["out"] = nc.dram_tensor("out", (S, D), F32, kind="ExternalOutput").ap()
    hybrid_layer(nc, **args)
    r = run_bass_kernel_spmd(nc, [{f"in_{k}": v for k, v in arrays.items()}], core_ids=[0])
    return r.results[0]["out"].reshape(1, S, D)
```

```python
import math
from contextlib import ExitStack

import numpy as np

import concourse.bass as bass
from concourse import mybir

F32 = mybir.dt.float32
F32R = mybir.dt.float32r
BF16 = mybir.dt.bfloat16
ALU = mybir.AluOpType
ACT = mybir.ActivationFunctionType
AX_X = mybir.AxisListType.X

P = 128
D = 1024
S = 256
NT = S // P
NK = D // P
RH, RD, RV = 4, 64, 128
MH, MD = 8, 64
MB = MH * MD // P
IN_COLS = 2 * RH * RD + 2 * RH * RV + 3 * MH * MD
DFF = -(-8 * D // (3 * 256)) * 256
EPS = 1e-6
BUCKETS, MAX_DIST = 32, 128
CW = 512
UNIT = 1024

RQK_COL, RV_COL, RG_COL, MQ_COL, MK_COL, MV_COL = range(6)
ORDER = [MQ_COL, MK_COL, MV_COL, RQK_COL, RV_COL, RG_COL]
NG = IN_COLS // CW
UPG = NK * CW // UNIT
KPU = UNIT // CW
N_IN = NG * UPG
WOUT_K = [4, 5, 6, 7, 0, 1, 2, 3]
N_OUT = len(WOUT_K)
FG = 256
NF = DFF // FG
GU = NK * 2 * FG // UNIT
DN = FG * D // (P * UNIT)
PER = GU + DN

RAW = 6
RING = 8
DRING = 4
HALVED = 4
WARM = 10
LEAD = 5
LO_UNITS = {16: [], 17: [21], 18: [22], 19: [23, 24]}
MASKED = 1e30
REV = 2 * P + S // 2

Q_T, K_T, S0, RQK_T = 6, 9, 10, 18
PT_LAG, PV_LAG = 2, 3
RS_SLOT = {19: [0], 20: [1, 2], 21: [3]}
RS_BANK = [0, 0, 1, 0]
RPV_SLOT = {21: [0, 1], 22: [2, 3]}
MIX_T = 22


def backwards(ap):
    *outer, (step, n) = [list(d) for d in ap.ap]
    return bass.AP(ap.tensor, ap.offset + (n - 1) * step, [*outer, [-step, n]])


def hybrid_layer(nc, xt, x, g_post_mix, g_pre_ffn, g_post_ffn, rel_bias,
                 w_in, w_out, w_gu, w_dn, ident_c, rope_c, decay_c, bucket_c, bias_row, out):
    with ExitStack() as ctx:
        def sb(name, shape, dt=F32, scope=ctx):
            return scope.enter_context(nc.sbuf_tensor(name, shape, dt))

        def sem(name):
            return ctx.enter_context(nc.semaphore(name))

        raw = sb("raw", [P, RAW, UNIT])
        w_hi = sb("w_hi", [P, RING, UNIT], F32R)
        w_lo = sb("w_lo", [P, RING, UNIT], F32R)
        a_hi = sb("a_hi", [P, NK, S], F32R)
        a_lo = sb("a_lo", [P, NK, S], F32R)
        m_hi = sb("m_hi", [P, NK, S], F32R)
        m_lo = sb("m_lo", [P, NK, S], F32R)
        xs = sb("xs", [P, NT, D])
        xg = sb("xg", [P, NT, D])
        gm = sb("gm", [P, D])
        gp = sb("gp", [P, D])
        gf = sb("gf", [P, D])
        junk = sb("junk", [P, CW])
        ident = sb("ident", [P, P])
        ms = sb("ms", [P, 4, NT, 2])
        va = sb("va", [P, 4, NT])
        rstd = sb("rstd", [P, 4, NT])
        nq = sb("nq", [P, NT])
        half = sb("half", [P, RH])
        warm = sb("warm", [P, RH])
        X_, MIX_, X1_, F_ = range(4)
        RET_ = 4
        FACTORS = [(what, t) for what in (X_, RET_, MIX_, X1_, F_) for t in range(NT)]

        with ExitStack() as attn:
            v = sb("v", [P, NT, CW], scope=attn)
            rv = sb("rv", [P, NT, CW], scope=attn)
            decay = sb("decay", [P, RH, 3 * P], scope=attn)
            rope = sb("rope", [P, NT, 3, RD // 2], scope=attn)
            lmin = sb("lmin", [P, NT, MH], scope=attn)
            esum = sb("esum", [P, NT, MH], scope=attn)
            erec = sb("erec", [P, NT, MH], scope=attn)
            rms4 = sb("rms4", [P, NT, RH], scope=attn)
            rs4 = sb("rs4", [P, NT, RH], scope=attn)
            with ExitStack() as early:
                qn = sb("qn", [P, NT, CW], scope=early)
                kn = sb("kn", [P, NT, CW], scope=early)
                xT = sb("xT", [P, NK + NK * S], scope=early)
                rel = sb("rel", [BUCKETS + 1, MH], scope=early)
                bucket = sb("bucket", [BUCKETS + 1, REV], scope=early)
                brow = sb("brow", [MH, REV], scope=early)
            with ExitStack() as late:
                rot = sb("rot", [P, NT, CW], scope=late)
                rot_b = sb("rot_b", [P, CW], scope=late)
                rT = sb("rT", [P, 4, S], scope=late)
                rs = sb("rs", [P, RH, 3 * P], scope=late)
                with ExitStack() as mid:
                    bias = sb("bias", [P, MH, S], scope=mid)
                    qT = sb("qT", [P, MB, S], scope=mid)
                    kT = sb("kT", [P, MB, S], scope=mid)
                    pr = sb("pr", [P, 3, 3 * P], scope=mid)
                    pT = sb("pT", [P, 2, 3 * P], scope=mid)
                with ExitStack() as tail:
                    ret = sb("ret", [P, NT, CW], scope=tail)
                    gate = sb("gate", [P, NT, CW], scope=tail)
                    mix = sb("mix", [P, NT, D], scope=tail)
        with ExitStack() as ffn:
            d_hi = sb("d_hi", [P, DRING, UNIT], F32R, scope=ffn)
            d_lo = sb("d_lo", [P, DRING, UNIT], F32R, scope=ffn)
            h_hi = sb("h_hi", [P, NT, DN, P], F32R, scope=ffn)
            h_lo = sb("h_lo", [P, NT, DN, P], F32R, scope=ffn)
            sil = sb("sil", [P, NT, FG], scope=ffn)
            hid = sb("hid", [P, NT, FG], scope=ffn)
            res = sb("res", [P, NT, D], scope=ffn)

        bank01 = ctx.enter_context(nc.psum_tensor("bank01", [P, 2, CW], F32))
        bank23 = ctx.enter_context(nc.psum_tensor("bank23", [P, 2, CW], F32))
        bank45 = ctx.enter_context(nc.psum_tensor("bank45", [P, 2, CW], F32))
        bank67 = ctx.enter_context(nc.psum_tensor("bank67", [P, 2, CW], F32))
        pj = [bank01, bank23]
        wk = bank45
        po = bank67
        ro = bank01
        pm = [bank67, bank23]
        ph = bank45
        pg = bank01
        pt = bank45
        pf = [bank67, bank23]

        raw_half = [sem(f"raw_half{i}") for i in range(HALVED)]
        raw_loaded = [sem(f"raw_loaded{i}") for i in range(RAW)]
        warmed = sem("warmed")
        zeros_ready = sem("zeros_ready")
        hi_half = sem("hi_half")
        lo_half = sem("lo_half")
        hi_ready = sem("hi_ready")
        lo_ready = sem("lo_ready")
        w_used = sem("w_used")
        d_used = sem("d_used")
        xt_loaded = [sem(f"xt_loaded{i}") for i in range(NK // KPU)]
        xt_first = sem("xt_first")
        x_loaded = [sem(f"x_loaded{t}") for t in range(NT)]
        gm_loaded = sem("gm_loaded")
        gp_loaded = sem("gp_loaded")
        gf_loaded = sem("gf_loaded")
        ident_loaded = sem("ident_loaded")
        rope_loaded = sem("rope_loaded")
        decay_loaded = sem("decay_loaded")
        rel_loaded = sem("rel_loaded")
        rel_one = sem("rel_one")
        brow_done = sem("brow_done")
        brow_ready = sem("brow_ready")
        brow_stored = sem("brow_stored")
        bias_loaded = sem("bias_loaded")
        x_hi = sem("x_hi")
        x_lo = sem("x_lo")
        sq_done = sem("sq_done")
        stat = sem("stat")
        var_ready = sem("var_ready")
        half_ready = sem("half_ready")
        rstd_ready = sem("rstd_ready")
        nq_ready = sem("nq_ready")
        proj_done = sem("proj_done")
        q_nat = sem("q_nat")
        k_nat = sem("k_nat")
        v_nat = sem("v_nat")
        rv_nat = sem("rv_nat")
        rot_ready = sem("rot_ready")
        gate_ready = sem("gate_ready")
        q_turned = sem("q_turned")
        k_turned = sem("k_turned")
        r_turned = sem("r_turned")
        qT_ready = sem("qT_ready")
        kT_ready = sem("kT_ready")
        rT_ready = sem("rT_ready")
        s_done = sem("s_done")
        l_ready = sem("l_ready")
        p_ready = sem("p_ready")
        pt_done = sem("pt_done")
        pT_ready = sem("pT_ready")
        pv_done = sem("pv_done")
        rs_done = sem("rs_done")
        rs_ready = sem("rs_ready")
        ro_done = sem("ro_done")
        sq4_done = sem("sq4_done")
        ret_ready = sem("ret_ready")
        mix_ready = sem("mix_ready")
        mix_turned = sem("mix_turned")
        mhi_ready = sem("mhi_ready")
        mlo_ready = sem("mlo_ready")
        wm_done = sem("wm_done")
        xg_ready = sem("xg_ready")
        hg_ready = sem("hg_ready")
        hg_turned = sem("hg_turned")
        ahi_ready = sem("ahi_ready")
        alo_ready = sem("alo_ready")
        mixg_ready = sem("mixg_ready")
        mixn_ready = sem("mixn_ready")
        x1_ready = sem("x1_ready")
        gu_done = sem("gu_done")
        sil_ready = [sem(f"sil_ready{t}") for t in range(NT)]
        hid_ready = [sem(f"hid_ready{t}") for t in range(NT)]
        h_turned = [sem(f"h_turned{t}") for t in range(NT)]
        hhi_ready = [sem(f"hhi_ready{t}") for t in range(NT)]
        hlo_ready = [sem(f"hlo_ready{t}") for t in range(NT)]
        dn_done = sem("dn_done")
        f_done = sem("f_done")
        res_part = sem("res_part")
        res_ready = sem("res_ready")
        out_stored = sem("out_stored")

        def gu_n(g, s):
            return N_IN + N_OUT + GU + PER * (g - 1) + s

        def dn_n(g, j):
            if isinstance(g, int) and g == NF - 1:
                return N_IN + N_OUT + GU + PER * g + j
            return N_IN + N_OUT + GU + PER * g + GU + j

        assert PER == RAW

        def squares_of(what, t, c):
            return NT * 2 * [X_, MIX_, X1_, F_].index(what) + 2 * t + c + 1

        def gain(k):
            return xT[:, k:k + 1]

        def x_block(k):
            return xT[:, NK + k * S:NK + (k + 1) * S]

        def wait_x_block(eng, k):
            if k == 0:
                eng.wait_ge(xt_first, 16)
            elif k == 1 or k % KPU == 0:
                eng.wait_ge(xt_loaded[k // KPU], 16)

        def wait_raw(eng, n, rounds=0):
            eng.wait_ge(raw_loaded[n % RAW], 16 * rounds + 16 * (n // RAW + 1))

        def wait_factor(eng, what, t):
            eng.wait_ge(rstd_ready, FACTORS.index((what, t)) + 1)

        def wait_projection(eng, group, t):
            if t == 0:
                eng.wait_ge(proj_done, group + 1)
            else:
                eng.wait_ge(w_used, UPG * (group + 1))

        def wait_mixer(eng, t, c):
            if (t, c) == (1, 1):
                eng.wait_ge(w_used, N_IN + N_OUT)
            else:
                eng.wait_ge(wm_done, 2 * t + c + 1)

        def wait_gate_up(eng, g, t):
            if t == 0:
                eng.wait_ge(gu_done, g + 1)
            else:
                eng.wait_ge(w_used, GU * g + (N_IN + N_OUT + GU))

        def wait_down(eng, g, t):
            if t == 0:
                eng.wait_ge(dn_done, g + 1)
            else:
                eng.wait_ge(d_used, DN * g + DN)

        block = ctx.enter_context(nc.Block())

        @block.sync
        def _(sp):
            def load(n, slot, src):
                if not (isinstance(n, int) and n < RAW):
                    sp.wait_ge(lo_ready, n - RAW + 1)
                sp.dma_start(raw[:, slot, :], src).then_inc(raw_loaded[slot], 16)

            def load_x(k0, k1, done):
                a, b = (NK + k0 * S if k0 else 0), NK + k1 * S
                sp.dma_start(xT[:, a:b], xt[:, a:b]).then_inc(done, 16)

            for n in range(N_IN):
                if 5 <= n < 5 + NT:
                    sp.dma_start(xs[:, n - 5, :], x[(n - 5) * P:(n - 4) * P, :]).then_inc(x_loaded[n - 5], 16)
                if n == 6:
                    sp.dma_start(ident[:, :], ident_c).then_inc(ident_loaded, 16)
                if n < HALVED:
                    for i in range(KPU):
                        sp.dma_start(raw[:, n, i * CW:(i + 1) * CW], w_in[n][:, i * CW:(i + 1) * CW]
                                     ).then_inc(raw_half[n] if i == 0 else raw_loaded[n], 16)
                        if n == 0:
                            load_x(i, i + 1, xt_first if i == 0 else xt_loaded[0])
                        elif i == 0:
                            load_x(KPU * n, KPU * (n + 1), xt_loaded[n])
                elif n < NK // KPU:
                    load_x(KPU * n, KPU * (n + 1), xt_loaded[n])
                    load(n, n % RAW, w_in[n])
                else:
                    load(n, n % RAW, w_in[n])
                if n == 12:
                    sp.dma_start(rope[:, :, :, :], rope_c).then_inc(rope_loaded, 16)
                if n == 15:
                    sp.dma_start(decay[:, :, :], decay_c).then_inc(decay_loaded, 16)
                if n == 16:
                    sp.dma_start(gp[:, :], g_pre_ffn.broadcast_to([P, D])).then_inc(gp_loaded, 16)
                if n == 18:
                    sp.dma_start(gm[:, :], g_post_mix.broadcast_to([P, D])).then_inc(gm_loaded, 16)
                if n == 20:
                    sp.dma_start(gf[:, :], g_post_ffn.broadcast_to([P, D])).then_inc(gf_loaded, 16)
            for i in range(N_OUT):
                load(N_IN + i, (N_IN + i) % RAW, w_out[i])
            base = N_IN + N_OUT
            for s in range(GU):
                load(base + s, (base + s) % RAW, w_gu[s])

            def group(g, n0):
                for s in range(GU):
                    load(gu_n(g, s), (n0 + s) % RAW, w_gu[GU * g + s])
                for j in range(DN):
                    load(dn_n(g - 1, j), (n0 + GU + j) % RAW, w_dn[DN * (g - 1) + j])

            group(1, gu_n(1, 0))
            group(2, gu_n(2, 0))
            with sp.Fori(3, NF - 1, 2) as g:
                group(g, gu_n(3, 0))
                group(g + 1, gu_n(4, 0))
            for j in range(DN):
                load(dn_n(NF - 1, j), dn_n(NF - 1, j) % RAW, w_dn[DN * (NF - 1) + j])

            for t in range(NT):
                for c in range(2):
                    sp.wait_ge(res_ready, 2 * t + c + 1)
                    sp.dma_start(out[t * P:(t + 1) * P, c * CW:(c + 1) * CW],
                                 res[:, t, c * CW:(c + 1) * CW]).then_inc(out_stored, 16)
            sp.wait_ge(out_stored, 16 * 2 * NT)

        @block.gpsimd
        def _(pool):
            def factor(i):
                what, t = FACTORS[i]
                src = rms4[:, t, :] if what == RET_ else va[:, what, t:t + 1]
                dst = rs4[:, t, :] if what == RET_ else rstd[:, what, t:t + 1]
                pool.wait_ge(var_ready, i + 1)
                pool.tensor_tensor(dst, src, half[:, 0:src.shape[1]], ALU.pow).then_inc(rstd_ready, 1)

            pool.memset(rel[BUCKETS:BUCKETS + 1, :], 1.0).then_inc(rel_one, 1)
            pool.wait_ge(rel_one, 1)
            pool.memset(half[:, :], -0.5).then_inc(half_ready, 1)
            pool.wait_ge(half_ready, 1)
            pool.dma_start(rel[0:BUCKETS, :], rel_bias).then_inc(rel_loaded, 16)
            pool.dma_start(bucket[:, :], bucket_c).then_inc(rel_loaded, 16)
            pool.wait_ge(brow_ready, 1)
            pool.dma_start(bias_row, brow[:, :]).then_inc(brow_stored, 16)
            for i in range(NT):
                factor(i)
            pool.wait_ge(brow_stored, 16)
            pool.wait_ge(x_lo, NK)
            pool.dma_start(bias[:, :, :], bass.AP(bias_row.tensor, 0, [[1, P], [REV, MH], [1, S]])
                           ).then_inc(bias_loaded, 16)
            pool.wait_ge(gp_loaded, 16)
            pool.wait_ge(gm_loaded, 16)
            for t in range(NT):
                pool.wait_ge(x_loaded[t], 16)
                pool.tensor_tensor(xg[:, t, :], xs[:, t, :], gp[:, :], ALU.mult).then_inc(xg_ready, 1)
            pool.wait_ge(xg_ready, NT)
            pool.tensor_tensor(gp[:, :], gm[:, :], gp[:, :], ALU.mult).then_inc(xg_ready, 1)
            for what in (RET_, MIX_):
                for t in range(NT):
                    factor(FACTORS.index((what, t)))
            for t in range(NT):
                for c in range(2):
                    cols = slice(c * CW, (c + 1) * CW)
                    pool.wait_ge(mixn_ready, 2 * t + c + 1)
                    pool.tensor_tensor(xs[:, t, cols], xs[:, t, cols], mix[:, t, cols], ALU.add
                                       ).then_inc(x1_ready, 1)
                factor(FACTORS.index((X1_, t)))
            for t in range(NT):
                factor(FACTORS.index((F_, t)))

        @block.scalar
        def _(act):
            def hi_in(n):
                wait_raw(act, n)
                if n >= RING:
                    act.wait_ge(w_used, n - RING + 1)
                act.activation(w_hi[:, n % RING, :], raw[:, n % RAW, :], ACT.Copy).then_inc(hi_ready, 1)

            squared = [0]

            def squares(what, t, c, src):
                if squared[0]:
                    act.wait_ge(sq_done, squared[0])
                squared[0] += 1
                act.activation(junk[:, 0:CW], src, ACT.Square, scale=1.0 / math.sqrt(D),
                               accum_out=ms[:, what, t, c:c + 1]).then_inc(sq_done, 1)

            act.wait_ge(half_ready, 1)
            act.activation(warm[:, :], half[:, :], ACT.Copy).then_inc(warmed, 1)
            for i in range(NK // KPU):
                for k in range(KPU * i, KPU * (i + 1)):
                    if i < HALVED:
                        cols = slice(k % KPU * CW, (k % KPU + 1) * CW)
                        if k % KPU == 0:
                            act.wait_ge(raw_half[i], 16)
                        else:
                            wait_raw(act, i)
                        act.activation(w_hi[:, i, cols], raw[:, i, cols], ACT.Copy
                                       ).then_inc(hi_half if k % KPU == 0 else hi_ready, 1)
                    wait_x_block(act, k)
                    act.activation(a_hi[:, k, :], x_block(k), ACT.Copy, scale=gain(k)).then_inc(x_hi, 1)
                if i >= HALVED:
                    hi_in(i)
            hi_in(4)

            def rows_out(dst, group, scale, done):
                for t in range(NT):
                    wait_projection(act, group, t)
                    act.activation(dst[:, t, :], pj[group % 2][:, t, :], ACT.Copy,
                                   scale=scale(t)).then_inc(done, 1)

            def turned_out(dst, src, turned, done, order=lambda ap: ap):
                for t in range(NT):
                    act.wait_ge(turned, t + 1)
                    act.activation(dst[:, :, t * P:(t + 1) * P],
                                   order(src[:, t, :].rearrange("p (b i) -> p b i", i=P)), ACT.Copy
                                   ).then_inc(done, 1)

            def r_x(t):
                return rstd[:, X_, t:t + 1]

            for u in range(N_IN):
                if 0 <= u - (S0 + 1) < MH:
                    h = u - (S0 + 1)
                    act.wait_ge(l_ready, h + 1)
                    for t, (a, b) in enumerate([(0, P), (P, 3 * P)]):
                        act.activation(pr[:, h % 3, a:b], pr[:, h % 3, a:b], ACT.Exp,
                                       bias=lmin[:, t, h:h + 1], scale=-1.0,
                                       accum_out=esum[:, t, h:h + 1]).then_inc(p_ready, 1)
                if u == Q_T + 1:
                    turned_out(qT, wk, q_turned, qT_ready, order=backwards)
                if u == K_T + 1:
                    turned_out(kT, wk, k_turned, kT_ready)
                hi_in(u + LEAD)
                if u == 0:
                    act.wait_ge(brow_done, 1)
                    act.activation(brow[:, :], wk[0:MH, 0, 0:REV], ACT.Copy).then_inc(brow_ready, 1)
                if u < NT:
                    act.wait_ge(w_used, 1)
                    act.wait_ge(x_loaded[u], 16)
                    for c in range(2):
                        squares(X_, u, c, xs[:, u, c * CW:(c + 1) * CW])
                if u == UPG:
                    act.wait_ge(nq_ready, 1)
                    wait_factor(act, X_, NT - 1)
                    rows_out(qn, 0, lambda t: nq[:, t:t + 1], q_nat)
                if u == 2 * UPG:
                    rows_out(kn, 1, r_x, k_nat)
                if u == 3 * UPG:
                    rows_out(v, 2, r_x, v_nat)
                if u == RQK_T + 1:
                    turned_out(rT, bank23, r_turned, rT_ready)
                if u == 5 * UPG:
                    rows_out(rv, 4, r_x, rv_nat)
                if u == MIX_T + 1:
                    for t, b in ((0, 1), (1, 0)):
                        act.wait_ge(mix_turned, t + 1)
                        act.activation(m_hi[:, 4:8, t * P:(t + 1) * P],
                                       backwards(wk[:, b, :].rearrange("p (b i) -> p b i", i=P)), ACT.Copy
                                       ).then_inc(mhi_ready, 1)
                    act.wait_ge(ro_done, RH)
                    for t in range(NT):
                        act.activation(ret[:, t, :], ro[:, t, :], ACT.Square, scale=1.0 / math.sqrt(RV)
                                       ).then_inc(sq4_done, 1)
            for t in range(NT):
                wait_projection(act, NG - 1, t)
                act.activation(gate[:, t, :], pj[1][:, t, :], ACT.Silu, scale=r_x(t)).then_inc(gate_ready, 1)
            for n in range(N_IN + LEAD, N_IN + N_OUT):
                hi_in(n)
            for t, b in ((0, 1), (1, 0)):
                act.wait_ge(mix_turned, NT + t + 1)
                act.activation(m_hi[:, 0:4, t * P:(t + 1) * P],
                               wk[:, b, :].rearrange("p (b i) -> p b i", i=P), ACT.Copy
                               ).then_inc(mhi_ready, 1)
            for s in range(GU):
                hi_in(N_IN + N_OUT + s)
            def mixer_squares(t, c):
                wait_mixer(act, t, c)
                squares(MIX_, t, c, pm[t][:, c, :])

            def a_hi_part(t, c):
                act.wait_ge(hg_turned, 2 * t + c + 1)
                act.activation(a_hi[:, 4 * c:4 * c + 4, t * P:(t + 1) * P],
                               ph[:, c, :].rearrange("p (b i) -> p b i", i=P), ACT.Copy
                               ).then_inc(ahi_ready, 1)

            def x1_squares(t):
                for c in range(2):
                    act.wait_ge(x1_ready, 2 * t + c + 1)
                    squares(X1_, t, c, xs[:, t, c * CW:(c + 1) * CW])

            mixer_squares(0, 0)
            mixer_squares(0, 1)
            mixer_squares(1, 0)
            a_hi_part(0, 0)
            mixer_squares(1, 1)
            a_hi_part(0, 1)

            def hi_gu(g, s, g0):
                n0 = gu_n(g0, s)
                wait_raw(act, n0, g - g0)
                a0 = N_IN + N_OUT + GU * g0 + s
                act.wait_ge(w_used, N_IN + N_OUT + GU * g + s - RING + 1)
                act.activation(w_hi[:, a0 % RING, :], raw[:, n0 % RAW, :], ACT.Copy).then_inc(hi_ready, 1)

            def hi_dn(g, j, g0):
                n0 = dn_n(g0, j)
                wait_raw(act, n0, g - g0)
                if not (isinstance(g, int) and DN * g + j < DRING):
                    act.wait_ge(d_used, DN * g + j - DRING + 1)
                act.activation(d_hi[:, (DN * g0 + j) % DRING, :], raw[:, n0 % RAW, :], ACT.Copy
                               ).then_inc(hi_ready, 1)

            def silu(g, t):
                wait_gate_up(act, g, t)
                if not (isinstance(g, int) and g == 0):
                    act.wait_ge(hid_ready[t], g)
                act.activation(sil[:, t, :], pg[:, t, 0:FG], ACT.Silu, scale=rstd[:, X1_, t:t + 1]
                               ).then_inc(sil_ready[t], 1)

            def h_hi_part(g, t):
                act.wait_ge(h_turned[t], g + 1)
                if not (isinstance(g, int) and g == 0):
                    wait_down(act, g - 1, t)
                act.activation(h_hi[:, t, :, :], pt[:, t, 0:FG].rearrange("p (b i) -> p b i", i=P),
                               ACT.Copy).then_inc(hhi_ready[t], 1)

            def group(g, g0, more=True):
                if more:
                    for s in range(GU - 1):
                        hi_gu(g + 1, s, g0 + 1)
                silu(g, 0)
                h_hi_part(g - 1, 1)
                if more:
                    hi_gu(g + 1, GU - 1, g0 + 1)
                for j in range(DN):
                    hi_dn(g, j, g0)
                silu(g, 1)
                h_hi_part(g, 0)

            hi_gu(1, 0, 1)
            a_hi_part(1, 0)
            hi_gu(1, 1, 1)
            a_hi_part(1, 1)
            x1_squares(0)
            hi_gu(1, 2, 1)
            wait_factor(act, X1_, 0)
            silu(0, 0)
            hi_gu(1, 3, 1)
            x1_squares(1)
            hi_dn(0, 0, 0)
            wait_factor(act, X1_, 1)
            silu(0, 1)
            h_hi_part(0, 0)
            hi_dn(0, 1, 0)
            group(1, 1)
            with act.Fori(2, NF - 2, 2) as g:
                group(g, 2)
                group(g + 1, 3)
            group(NF - 1, NF - 1, more=False)
            h_hi_part(NF - 1, 1)
            for t in range(NT):
                for c in range(2):
                    act.wait_ge(f_done, 2 * t + c + 1)
                    squares(F_, t, c, pf[t][:, c, :])

        @block.vector
        def _(dve):
            steps = [0]

            def small(ins):
                steps[0] += 1
                ins.then_inc(stat, 1)
                dve.wait_ge(stat, steps[0])

            def lo_in(n):
                dve.wait_ge(hi_ready, n + 1)
                dve.tensor_tensor(w_lo[:, n % RING, :], raw[:, n % RAW, :],
                                  w_hi[:, n % RING, :].bitcast(F32), ALU.subtract).then_inc(lo_ready, 1)

            def factor(what, t):
                dve.wait_ge(sq_done, squares_of(what, t, 1))
                dve.tensor_scalar(va[:, what, t:t + 1], ms[:, what, t, 0:1], ms[:, what, t, 1:2], EPS,
                                  ALU.add, ALU.add).then_inc(var_ready, 1)

            dve.memset(junk[:, 0:CW // 2], 0.0).then_inc(zeros_ready, 1)
            for i in range(NK // KPU):
                for k in range(KPU * i, KPU * (i + 1)):
                    if i < HALVED:
                        cols = slice(k % KPU * CW, (k % KPU + 1) * CW)
                        dve.wait_ge(hi_half if k % KPU == 0 else hi_ready, i + 1)
                        dve.tensor_tensor(w_lo[:, i, cols], raw[:, i, cols], w_hi[:, i, cols].bitcast(F32),
                                          ALU.subtract).then_inc(lo_half if k % KPU == 0 else lo_ready, 1)
                    wait_x_block(dve, k)
                    dve.wait_ge(x_hi, k + 1)
                    dve.scalar_tensor_tensor(out=a_lo[:, k, :], in0=x_block(k), scalar=gain(k),
                                             in1=a_hi[:, k, :].bitcast(F32), op0=ALU.mult,
                                             op1=ALU.subtract).then_inc(x_lo, 1)
                if i >= HALVED:
                    lo_in(i)
            lo_in(4)

            def rotary(t):
                half = RD // 2
                r = rstd[:, X_, t:t + 1]
                src = pj[1][:, t, :].rearrange("p (n d) -> p n d", d=half)
                halves = pj[1][:, t, :].rearrange("p (n a d) -> p n a d", a=2, d=half)
                turned = rot_b[:, :].rearrange("p (n a d) -> p n a d", a=2, d=half)

                def table(i, n):
                    return rope[:, t, i:i + 1, :].broadcast_to([P, n, half])

                wait_projection(dve, 3, t)
                dve.scalar_tensor_tensor(out=rot[:, t, :].rearrange("p (n d) -> p n d", d=half), in0=src,
                                         scalar=r, in1=table(0, 4 * RH), op0=ALU.mult, op1=ALU.mult)
                dve.scalar_tensor_tensor(out=turned[:, :, 0, :], in0=halves[:, :, 1, :], scalar=r,
                                         in1=table(2, 2 * RH), op0=ALU.mult, op1=ALU.mult)
                small(dve.scalar_tensor_tensor(out=turned[:, :, 1, :], in0=halves[:, :, 0, :], scalar=r,
                                               in1=table(1, 2 * RH), op0=ALU.mult, op1=ALU.mult))
                dve.tensor_tensor(rot[:, t, :], rot[:, t, :], rot_b[:, :], ALU.add).then_inc(rot_ready, 1)
                dve.wait_ge(rot_ready, t + 1)

            def logits(h):
                dve.wait_ge(s_done, h + 1)
                if h >= 3:
                    dve.wait_ge(pt_done, h - 2)
                for t, (a, b) in enumerate([(0, P), (P, 3 * P)]):
                    ins = dve.tensor_tensor_reduce(out=pr[:, h % 3, a:b], in0=wk[:, 0, a:b],
                                                   in1=bias[:, h, P - t * P:S], scale=1.0,
                                                   scalar=3.0e38, op0=ALU.add, op1=ALU.min,
                                                   accum_out=lmin[:, t, h:h + 1])
                ins.then_inc(l_ready, 1)

            for u in range(N_IN):
                if 0 <= u - (S0 + 1) < MH:
                    if u == S0 + 1:
                        dve.wait_ge(bias_loaded, 16)
                    logits(u - (S0 + 1))
                if 0 <= u - (S0 + PT_LAG + 1) < MH:
                    h = u - (S0 + PT_LAG + 1)
                    dve.wait_ge(pt_done, h + 1)
                    if h >= 2:
                        dve.wait_ge(pv_done, h - 1)
                    dve.tensor_copy(pT[:, h % 2, :], wk[:, 1, 0:3 * P]).then_inc(pT_ready, 1)
                if u == 4 * UPG:
                    dve.wait_ge(rope_loaded, 16)
                    rotary(0)
                if u == 4 * UPG + 1:
                    rotary(1)
                if u <= S0 + PT_LAG + MH:
                    for n in LO_UNITS.get(u, [u + LEAD]):
                        lo_in(n)
                if u < NT:
                    factor(X_, u)
                if u == NT:
                    wait_factor(dve, X_, NT - 1)
                    dve.tensor_scalar(nq[:, :], rstd[:, X_, :], -1.0 / math.sqrt(MD), None, ALU.mult
                                      ).then_inc(nq_ready, 1)
                for h in RS_SLOT.get(u - 1, []):
                    if h == 0:
                        dve.wait_ge(decay_loaded, 16)
                    dve.wait_ge(rs_done, h + 1)
                    dve.tensor_tensor(rs[:, h, :], wk[:, RS_BANK[h], 0:3 * P], decay[:, h, :], ALU.mult
                                      ).then_inc(rs_ready, 1)
                if u == S0 + PV_LAG + MH:
                    dve.wait_ge(p_ready, NT * MH)
                    small(dve.reciprocal(erec[:, :, :], esum[:, :, :]))
                    dve.wait_ge(pv_done, MH)
                    for t in range(NT):
                        dve.tensor_tensor(mix[:, t, CW:D].rearrange("p (h e) -> p h e", e=MD),
                                          po[:, t, :].rearrange("p (h e) -> p h e", e=MD),
                                          erec[:, t, :].unsqueeze(2).broadcast_to([P, MH, MD]),
                                          ALU.mult).then_inc(mix_ready, 1)
                if u > S0 + PT_LAG + MH:
                    lo_in(u + LEAD)
                if u == MIX_T + 1:
                    for t, b in ((0, 1), (1, 0)):
                        dve.wait_ge(mhi_ready, t + 1)
                        dve.tensor_tensor(m_lo[:, 4:8, t * P:(t + 1) * P],
                                          backwards(wk[:, b, :].rearrange("p (b i) -> p b i", i=P)),
                                          m_hi[:, 4:8, t * P:(t + 1) * P].bitcast(F32), ALU.subtract
                                          ).then_inc(mlo_ready, 1)
                    for t in range(NT):
                        dve.wait_ge(sq4_done, t + 1)
                        small(dve.tensor_reduce(rms4[:, t, :],
                                                ret[:, t, :].rearrange("p (h e) -> p h e", e=RV),
                                                AX_X, ALU.add))
                        dve.tensor_scalar(rms4[:, t, :], rms4[:, t, :], EPS, None, ALU.add
                                          ).then_inc(var_ready, 1)
                    for t in range(NT):
                        wait_factor(dve, RET_, t)
                        dve.tensor_tensor(ret[:, t, :].rearrange("p (h e) -> p h e", e=RV),
                                          ro[:, t, :].rearrange("p (h e) -> p h e", e=RV),
                                          rs4[:, t, :].unsqueeze(2).broadcast_to([P, RH, RV]),
                                          ALU.mult).then_inc(ret_ready, 1)
            for t in range(NT):
                dve.wait_ge(gate_ready, t + 1)
                dve.wait_ge(ret_ready, t + 1)
                dve.tensor_tensor(mix[:, t, 0:CW], ret[:, t, :], gate[:, t, :], ALU.mult
                                  ).then_inc(mix_ready, 1)
            for n in range(N_IN + LEAD, N_IN + N_OUT):
                lo_in(n)
            for t, b in ((0, 1), (1, 0)):
                dve.wait_ge(mhi_ready, NT + t + 1)
                dve.tensor_tensor(m_lo[:, 0:4, t * P:(t + 1) * P],
                                  wk[:, b, :].rearrange("p (b i) -> p b i", i=P),
                                  m_hi[:, 0:4, t * P:(t + 1) * P].bitcast(F32), ALU.subtract
                                  ).then_inc(mlo_ready, 1)
            for s in range(GU):
                lo_in(N_IN + N_OUT + s)

            def scaled(t):
                if t == 0:
                    dve.wait_ge(xg_ready, NT + 1)
                for c in range(2):
                    cols = slice(c * CW, (c + 1) * CW)
                    if c == 0:
                        dve.wait_ge(sq_done, squares_of(MIX_, t, 0))
                    else:
                        if t == 1:
                            a_lo_part(0, 0)
                        factor(MIX_, t)
                        if t == 1:
                            a_lo_part(0, 1)
                    dve.tensor_tensor(mix[:, t, cols], pm[t][:, c, :], gp[:, cols], ALU.mult
                                      ).then_inc(mixg_ready, 1)
                wait_factor(dve, MIX_, t)
                dve.wait_ge(mixg_ready, 2 * t + 2)
                for c in range(2):
                    cols = slice(c * CW, (c + 1) * CW)
                    dve.scalar_tensor_tensor(out=xg[:, t, cols], in0=mix[:, t, cols],
                                             scalar=rstd[:, MIX_, t:t + 1], in1=xg[:, t, cols],
                                             op0=ALU.mult, op1=ALU.add).then_inc(hg_ready, 1)

            def a_lo_part(t, c):
                dve.wait_ge(ahi_ready, 2 * t + c + 1)
                dve.tensor_tensor(a_lo[:, 4 * c:4 * c + 4, t * P:(t + 1) * P],
                                  ph[:, c, :].rearrange("p (b i) -> p b i", i=P),
                                  a_hi[:, 4 * c:4 * c + 4, t * P:(t + 1) * P].bitcast(F32), ALU.subtract
                                  ).then_inc(alo_ready, 1)

            def residual(t):
                for c in range(2):
                    cols = slice(c * CW, (c + 1) * CW)
                    dve.scalar_tensor_tensor(out=mix[:, t, cols], in0=pm[t][:, c, :],
                                             scalar=rstd[:, MIX_, t:t + 1], in1=gm[:, cols],
                                             op0=ALU.mult, op1=ALU.mult).then_inc(mixn_ready, 1)

            dve.wait_ge(gm_loaded, 16)
            scaled(0)
            scaled(1)

            def lo_gu(g, s, g0):
                n0 = gu_n(g0, s)
                slot = (N_IN + N_OUT + GU * g0 + s) % RING
                dve.wait_ge(hi_ready, gu_n(g, s) + 1)
                dve.tensor_tensor(w_lo[:, slot, :], raw[:, n0 % RAW, :], w_hi[:, slot, :].bitcast(F32),
                                  ALU.subtract).then_inc(lo_ready, 1)

            def lo_dn(g, j, g0):
                n0 = dn_n(g0, j)
                slot = (DN * g0 + j) % DRING
                dve.wait_ge(hi_ready, dn_n(g, j) + 1)
                dve.tensor_tensor(d_lo[:, slot, :], raw[:, n0 % RAW, :], d_hi[:, slot, :].bitcast(F32),
                                  ALU.subtract).then_inc(lo_ready, 1)

            def hidden(g, t):
                dve.wait_ge(sil_ready[t], g + 1)
                if not (isinstance(g, int) and g == 0):
                    dve.wait_ge(h_turned[t], g)
                dve.scalar_tensor_tensor(out=hid[:, t, :], in0=pg[:, t, FG:2 * FG],
                                         scalar=rstd[:, X1_, t:t + 1], in1=sil[:, t, :],
                                         op0=ALU.mult, op1=ALU.mult).then_inc(hid_ready[t], 1)

            def h_lo_part(g, t):
                dve.wait_ge(hhi_ready[t], g + 1)
                dve.tensor_tensor(h_lo[:, t, :, :], pt[:, t, 0:FG].rearrange("p (b i) -> p b i", i=P),
                                  h_hi[:, t, :, :].bitcast(F32), ALU.subtract).then_inc(hlo_ready[t], 1)

            def group(g, g0, more=True):
                if more:
                    for s in range(GU - 1):
                        lo_gu(g + 1, s, g0 + 1)
                hidden(g, 0)
                h_lo_part(g - 1, 1)
                if more:
                    lo_gu(g + 1, GU - 1, g0 + 1)
                for j in range(DN):
                    lo_dn(g, j, g0)
                hidden(g, 1)
                h_lo_part(g, 0)

            residual(0)
            a_lo_part(1, 0)
            lo_gu(1, 0, 1)
            a_lo_part(1, 1)
            residual(1)
            factor(X1_, 0)
            lo_gu(1, 1, 1)
            hidden(0, 0)
            lo_gu(1, 2, 1)
            lo_gu(1, 3, 1)
            factor(X1_, 1)
            lo_dn(0, 0, 0)
            hidden(0, 1)
            h_lo_part(0, 0)
            lo_dn(0, 1, 0)
            group(1, 1)
            with dve.Fori(2, NF - 2, 2) as g:
                group(g, 2)
                group(g + 1, 3)
            group(NF - 1, NF - 1, more=False)
            h_lo_part(NF - 1, 1)
            dve.wait_ge(gf_loaded, 16)
            for t in range(NT):
                for c in range(2):
                    cols = slice(c * CW, (c + 1) * CW)
                    if c == 0:
                        dve.wait_ge(sq_done, squares_of(F_, t, 0))
                    else:
                        factor(F_, t)
                    dve.tensor_tensor(res[:, t, cols], pf[t][:, c, :], gf[:, cols], ALU.mult
                                      ).then_inc(res_part, 1)
                wait_factor(dve, F_, t)
                dve.wait_ge(res_part, 2 * t + 2)
                for c in range(2):
                    cols = slice(c * CW, (c + 1) * CW)
                    dve.scalar_tensor_tensor(out=res[:, t, cols], in0=res[:, t, cols],
                                             scalar=rstd[:, F_, t:t + 1], in1=xs[:, t, cols],
                                             op0=ALU.mult, op1=ALU.add).then_inc(res_ready, 1)

        @block.tensor
        def _(pe):
            def product(acc, hi, lo, wh, wl, first, last):
                pe.matmul(acc, hi, wh, start=first, stop=False)
                pe.matmul(acc, hi, wl, start=False, stop=False)
                return pe.matmul(acc, lo, wh, start=False, stop=last)

            def tile(t):
                return slice(t * P, (t + 1) * P)

            def turn(dst, src, blocks, done):
                for b in range(blocks):
                    ins = pe.transpose(dst[:, b * P:(b + 1) * P], src[:, b * P:(b + 1) * P], ident[:, :])
                ins.then_inc(done, 1)

            zeros = junk[:, 0:CW // 2].bitcast(BF16)
            pe.wait_ge(zeros_ready, 1)
            for _ in range(WARM):
                pe.matmul(bank67[:, 0, :], zeros[:, 0:P], zeros[:, 0:CW], start=True, stop=True)

            def first_unit(u):
                for i in range(KPU):
                    k, cols = KPU * u + i, slice(i * CW, (i + 1) * CW)
                    pe.wait_ge(hi_half if i == 0 else hi_ready, u + 1)
                    pe.wait_ge(x_hi, k + 1)
                    for t in range(NT):
                        pe.matmul(pj[0][:, t, :], a_hi[:, k, tile(t)], w_hi[:, u, cols],
                                  start=(k == 0), stop=False)
                    pe.wait_ge(lo_half if i == 0 else lo_ready, u + 1)
                    for t in range(NT):
                        pe.matmul(pj[0][:, t, :], a_hi[:, k, tile(t)], w_lo[:, u, cols],
                                  start=False, stop=False)
                    pe.wait_ge(x_lo, k + 1)
                    for t in range(NT):
                        ins = pe.matmul(pj[0][:, t, :], a_lo[:, k, tile(t)], w_hi[:, u, cols],
                                        start=False, stop=(k == NK - 1))
                        if t == 0 and k == NK - 1:
                            ins.then_inc(proj_done, 1)
                ins.then_inc(w_used, 1)

            def head_rows(h):
                return slice(64 * (h % 2), 64 * (h % 2) + 64)

            for u in range(N_IN):
                g, s = divmod(u, UPG)
                if u < HALVED:
                    first_unit(u)
                else:
                    pe.wait_ge(lo_ready, u + 1)
                for t in range(0 if u < HALVED else NT):
                    if s == 0:
                        if g == 2:
                            pe.wait_ge(q_nat, t + 1)
                        if g == 3:
                            pe.wait_ge(k_nat, t + 1)
                        if g == 4:
                            pe.wait_ge(v_nat, t + 1)
                        if g == 5:
                            pe.wait_ge(rT_ready, t + 1)
                    for i in range(KPU):
                        k = KPU * s + i
                        if g == 0 and t == 0:
                            pe.wait_ge(x_lo, k + 1)
                        ins = product(pj[g % 2][:, t, :], a_hi[:, k, tile(t)], a_lo[:, k, tile(t)],
                                      w_hi[:, u % RING, i * CW:(i + 1) * CW],
                                      w_lo[:, u % RING, i * CW:(i + 1) * CW],
                                      first=(k == 0), last=(k == NK - 1))
                    if s == UPG - 1 and t == 0:
                        ins.then_inc(proj_done, 1)
                if u >= HALVED:
                    ins.then_inc(w_used, 1)

                if u == 1:
                    pe.wait_ge(rel_one, 1)
                    pe.wait_ge(rel_loaded, 32)
                    pe.matmul(wk[0:MH, 0, 0:REV], rel[:, :], bucket[:, :], start=True, stop=True
                              ).then_inc(brow_done, 1)
                if u == Q_T:
                    pe.wait_ge(ident_loaded, 16)
                    pe.wait_ge(brow_ready, 1)
                    for t in range(NT):
                        pe.wait_ge(q_nat, t + 1)
                        turn(wk[:, t, :], qn[:, t, :], MB, q_turned)
                if u == K_T:
                    for t in range(NT):
                        pe.wait_ge(k_nat, t + 1)
                        pe.wait_ge(qT_ready, t + 1)
                        turn(wk[:, t, :], kn[:, t, :], MB, k_turned)
                if 0 <= u - S0 < MH:
                    h = u - S0
                    rows, b = head_rows(h), h // 2
                    if h == 0:
                        pe.wait_ge(kT_ready, NT)
                    else:
                        pe.wait_ge(l_ready, h)
                    pe.matmul(wk[:, 0, 0:P], qT[rows, b, tile(0)], kT[rows, b, tile(0)],
                              start=True, stop=True)
                    pe.matmul(wk[:, 0, P:3 * P], qT[rows, b, tile(1)], kT[rows, b, :],
                              start=True, stop=True).then_inc(s_done, 1)
                if 0 <= u - (S0 + PT_LAG) < MH:
                    h = u - (S0 + PT_LAG)
                    pe.wait_ge(p_ready, NT * (h + 1))
                    if h > 0:
                        pe.wait_ge(pT_ready, h)
                    turn(wk[:, 1, :], pr[:, h % 3, :], 3, pt_done)
                if 0 <= u - (S0 + PV_LAG) < MH:
                    h = u - (S0 + PV_LAG)
                    cols = slice(h * MD, (h + 1) * MD)
                    pe.wait_ge(pT_ready, h + 1)
                    if h == 0:
                        pe.wait_ge(v_nat, NT)
                    pe.matmul(po[:, 0, cols], pT[:, h % 2, 0:P], v[:, 0, cols], start=True, stop=True)
                    pe.matmul(po[:, 1, cols], pT[:, h % 2, P:2 * P], v[:, 0, cols], start=True, stop=False)
                    pe.matmul(po[:, 1, cols], pT[:, h % 2, 2 * P:3 * P], v[:, 1, cols],
                              start=False, stop=True).then_inc(pv_done, 1)
                if u == RQK_T:
                    for t in range(NT):
                        pe.wait_ge(rot_ready, t + 1)
                        turn(bank23[:, t, :], rot[:, t, :], 4, r_turned)
                for h in RS_SLOT.get(u, []):
                    rows, b = head_rows(h), h // 2
                    if h == 0:
                        pe.wait_ge(rT_ready, NT)
                        pe.wait_ge(l_ready, MH)
                    elif h == 2:
                        pe.wait_ge(pT_ready, MH)
                    else:
                        pe.wait_ge(rs_ready, 1 if h == 1 else 2)
                    pe.matmul(wk[:, RS_BANK[h], 0:2 * P], rT[rows, 2 + b, tile(0)], rT[rows, b, :],
                              start=True, stop=True)
                    pe.matmul(wk[:, RS_BANK[h], 2 * P:3 * P], rT[rows, 2 + b, tile(1)],
                              rT[rows, b, tile(1)], start=True, stop=True).then_inc(rs_done, 1)
                for h in RPV_SLOT.get(u, []):
                    cols = slice(h * RV, (h + 1) * RV)
                    if h == 0:
                        pe.wait_ge(rv_nat, NT)
                    pe.wait_ge(rs_ready, h + 1)
                    pe.matmul(ro[:, 0, cols], rs[:, h, 0:P], rv[:, 0, cols], start=True, stop=True)
                    pe.matmul(ro[:, 1, cols], rs[:, h, P:2 * P], rv[:, 0, cols], start=True, stop=False)
                    pe.matmul(ro[:, 1, cols], rs[:, h, 2 * P:3 * P], rv[:, 1, cols],
                              start=False, stop=True).then_inc(ro_done, 1)
                if u == MIX_T:
                    for t, b in ((0, 1), (1, 0)):
                        pe.wait_ge(mix_ready, t + 1)
                        pe.wait_ge(rs_ready, 3 if b else 4)
                        turn(wk[:, b, :], mix[:, t, CW:D], 4, mix_turned)

            def mixer(t, part, c, between=None):
                for i in range(4 * part, 4 * part + 4):
                    k, n = WOUT_K[i], N_IN + i
                    if t == 0:
                        pe.wait_ge(lo_ready, n + 1)
                    ins = product(pm[t][:, c, :], m_hi[:, k, tile(t)], m_lo[:, k, tile(t)],
                                  w_hi[:, n % RING, c * CW:(c + 1) * CW],
                                  w_lo[:, n % RING, c * CW:(c + 1) * CW],
                                  first=(i == 0), last=(i == N_OUT - 1))
                    if t == 1 and c == 1:
                        ins.then_inc(w_used, 1)
                    if between and i == 4 * part + 1:
                        between()
                return ins

            for t, b in ((0, 1), (1, 0)):
                pe.wait_ge(mlo_ready, t + 1)
                if t == 1:
                    pe.wait_ge(gate_ready, NT)
                for c in range(2):
                    mixer(t, 0, c)
                pe.wait_ge(mix_ready, NT + t + 1)
                pe.wait_ge(mlo_ready, t + 1)
                turn(wk[:, b, :], mix[:, t, 0:CW], 4, mix_turned)
            pe.wait_ge(mlo_ready, NT + 1)
            for c in range(2):
                mixer(0, 1, c).then_inc(wm_done, 1)
            pe.wait_ge(mlo_ready, 2 * NT)

            def turn_scaled(t, c):
                pe.wait_ge(hg_ready, 2 * t + c + 1)
                if t == 1:
                    pe.wait_ge(alo_ready, c + 1)
                turn(ph[:, c, :], xg[:, t, c * CW:(c + 1) * CW], 4, hg_turned)

            mixer(1, 1, 0).then_inc(wm_done, 1)
            mixer(1, 1, 1, between=lambda: turn_scaled(0, 0))
            turn_scaled(0, 1)

            def gate_up(g, t, g0, hook=None):
                if not (isinstance(g, int) and g == 0):
                    pe.wait_ge(hid_ready[t], g)
                for s in range(GU):
                    a0 = N_IN + N_OUT + GU * g0 + s
                    if t == 0:
                        pe.wait_ge(lo_ready, (gu_n(g, s) if g0 else N_IN + N_OUT + s) + 1)
                    for i in range(KPU):
                        k = KPU * s + i
                        if g0 == 0 and k % 4 == 0:
                            pe.wait_ge(alo_ready, 2 * t + k // 4 + 1)
                        ins = product(pg[:, t, :], a_hi[:, k, tile(t)], a_lo[:, k, tile(t)],
                                      w_hi[:, a0 % RING, i * CW:(i + 1) * CW],
                                      w_lo[:, a0 % RING, i * CW:(i + 1) * CW],
                                      first=(k == 0), last=(k == NK - 1))
                    if t == 1:
                        ins.then_inc(w_used, 1)
                    elif s == GU - 1:
                        ins.then_inc(gu_done, 1)
                    if hook:
                        hook(s)

            def turn_hidden(g, t):
                pe.wait_ge(hid_ready[t], g + 1)
                if not (isinstance(g, int) and g == 0):
                    pe.wait_ge(hlo_ready[t], g)
                turn(pt[:, t, :], hid[:, t, :], DN, h_turned[t])

            def down(g, t, g0, last=False):
                pe.wait_ge(hlo_ready[t], g + 1)
                if g0 == 0:
                    pe.wait_ge(x1_ready, 2 * t + 2)
                for c in range(2):
                    for j in range(DN):
                        slot = (DN * g0 + j) % DRING
                        if t == 0 and c == 0:
                            pe.wait_ge(lo_ready, dn_n(g, j) + 1)
                        ins = product(pf[t][:, c, :], h_hi[:, t, j, :], h_lo[:, t, j, :],
                                      d_hi[:, slot, c * CW:(c + 1) * CW],
                                      d_lo[:, slot, c * CW:(c + 1) * CW],
                                      first=(g0 == 0 and j == 0), last=(last and j == DN - 1))
                        if t == 1 and c == 1 and not last:
                            ins.then_inc(d_used, 1)
                    if last:
                        ins.then_inc(f_done, 1)
                if t == 0 and not last:
                    ins.then_inc(dn_done, 1)

            def group(g, g0):
                gate_up(g, 0, g0)
                turn_hidden(g - 1, 1)
                down(g - 1, 0, g0 - 1)
                gate_up(g, 1, g0)
                turn_hidden(g, 0)
                down(g - 1, 1, g0 - 1)

            def scaled_hook(s):
                if s >= 2:
                    turn_scaled(1, s - 2)

            gate_up(0, 0, 0, hook=scaled_hook)
            gate_up(0, 1, 0)
            turn_hidden(0, 0)
            group(1, 1)
            with pe.Fori(2, NF - 2, 2) as g:
                group(g, 2)
                group(g + 1, 3)
            group(NF - 1, NF - 1)
            turn_hidden(NF - 1, 1)
            down(NF - 1, 0, NF - 1, last=True)
            down(NF - 1, 1, NF - 1, last=True)


def _bucket(n):
    exact = BUCKETS // 2
    far = exact + (np.log(np.maximum(n, 1).astype(np.float32) / np.float32(exact))
                   / np.float32(math.log(MAX_DIST / exact)) * np.float32(BUCKETS - exact)).astype(np.int32)
    return np.where(n < exact, n, np.minimum(far, BUCKETS - 1))


def _constants():
    ident = np.eye(P, dtype=np.float32)
    half = RD // 2
    inv = np.float32(10000.0) ** (-np.arange(half, dtype=np.float32) / np.float32(half))
    ang = (np.arange(S, dtype=np.float32)[:, None] * inv[None, :]).astype(np.float32).astype(np.float64)
    rope = np.stack([np.cos(ang), np.sin(ang), -np.sin(ang)], 1).astype(np.float32)
    rope = np.ascontiguousarray(rope.reshape(NT, P, 3, half).transpose(1, 0, 2, 3))
    log_gamma = np.log1p(-np.exp(np.linspace(math.log(1.0 / 32), math.log(1.0 / 512), RH)))
    j = np.arange(P)[:, None]
    dist = np.concatenate([np.arange(S)[None, :] - j, np.arange(P)[None, :] - j], 1)
    decay = np.where(dist >= 0, np.exp(np.maximum(dist, 0)[None] * log_gamma[:, None, None]), 0.0) * RD ** -0.5
    decay = np.ascontiguousarray(decay.transpose(1, 0, 2)).astype(np.float32)
    n = S - 1 - np.arange(REV)
    bucket = np.zeros((BUCKETS + 1, REV), np.float32)
    past = n >= 0
    bucket[_bucket(np.maximum(n, 0))[past], np.arange(REV)[past]] = -1.0
    bucket[BUCKETS, ~past] = MASKED
    return {"ident_c": ident, "rope_c": rope, "decay_c": decay, "bucket_c": bucket}


def _laid_out(i):
    def a(name):
        return np.asarray(i[name])

    x = a("x")[0]
    w_in = a("w_in")[0].reshape(UPG, KPU, P, NG, CW)[:, :, :, ORDER]
    gate = a("w_gate")[0].reshape(GU, KPU, P, NF, FG)
    up = a("w_up")[0].reshape(GU, KPU, P, NF, FG)
    return {
        "xt": np.concatenate([a("pre_mix_norm")[0].reshape(NK, P).T,
                              x.T.reshape(NK, P, S).transpose(1, 0, 2).reshape(P, NK * S)], 1),
        "x": x,
        "g_post_mix": a("post_mix_norm"),
        "g_pre_ffn": a("pre_ffn_norm"),
        "g_post_ffn": a("post_ffn_norm"),
        "rel_bias": a("rel_bias"),
        "w_in": w_in.transpose(3, 0, 2, 1, 4).reshape(N_IN, P, UNIT),
        "w_out": a("w_out")[0].reshape(NK, P, D)[WOUT_K],
        "w_gu": np.stack([gate, up], 4).transpose(3, 0, 2, 1, 4, 5).reshape(NF * GU, P, UNIT),
        "w_dn": a("w_down")[0].reshape(NF * DN, P, D),
    }


def kernel(**inputs):
    import concourse.bacc as bacc
    from concourse.bass_utils import run_bass_kernel_spmd

    arrays = {k: np.ascontiguousarray(v) for k, v in {**_laid_out(inputs), **_constants()}.items()}
    nc = bacc.Bacc("TRN2", target_bir_lowering=False, num_devices=1)
    args = {k: nc.dram_tensor(f"in_{k}", v.shape, mybir.dt.from_np(v.dtype), kind="ExternalInput").ap()
            for k, v in arrays.items()}
    args["bias_row"] = nc.dram_tensor("bias_row", (MH, REV), F32, kind="Internal").ap()
    args["out"] = nc.dram_tensor("out", (S, D), F32, kind="ExternalOutput").ap()
    hybrid_layer(nc, **args)
    r = run_bass_kernel_spmd(nc, [{f"in_{k}": v for k, v in arrays.items()}], core_ids=[0])
    return r.results[0]["out"].reshape(1, S, D)
```
